# Optimizing a Trainium2 kernel written in Bass

```python
import jax, jax.numpy as jnp
from jax import lax
import numpy as np
import math

D_MODEL = 1024
BATCH = 1
SEQ = 1024
DEPTH = 1

HEAD_DIM = 64
D_A = D_MODEL // 4
D_B = 3 * D_MODEL // 8
D_C = 3 * D_MODEL // 8
D_MIX = D_A + D_B + D_C
N_HEADS_A = D_A // HEAD_DIM
N_BLOCKS_B = D_B // HEAD_DIM
N_HEADS_C = D_C // HEAD_DIM
CHUNK = 128
CONV_B = 4
LRU_C = 8.0
LORA_W = 64
LORA_A = 64
LORA_G = 128
D_FF = 2816
CONV_FF = 3
N_MOD = 6
EPS = 1e-6
LN_EPS = 1e-5
GN_EPS = 64e-5
P_A = 2 * D_A
P_B = 2 * D_B
P_C = 3 * D_C + LORA_W + LORA_A + LORA_G
P_IN = P_A + P_B + P_C


def rms_norm(x, g):
    xf = x.astype(jnp.float32)
    y = xf * lax.rsqrt(jnp.mean(xf * xf, axis=-1, keepdims=True) + EPS)
    return (y * g.astype(jnp.float32)).astype(x.dtype)

def causal_dwconv(x, w, b):
    k_w = w.shape[0]
    s = x.shape[1]
    xp = jnp.pad(x, ((0, 0), (k_w - 1, 0), (0, 0)))
    y = b + w[0] * xp[:, 0:s]
    for j in range(1, k_w):
        y = y + w[j] * xp[:, j:j + s]
    return y

def token_shift(x):
    return jnp.pad(x[:, :-1], ((0, 0), (1, 0), (0, 0)))

def chunked_sgu(p, ln_g, ln_b, w_s, b_s):
    z = jax.nn.gelu(p)
    u, v = jnp.split(z, 2, axis=-1)
    vf = v.astype(jnp.float32)
    mu = jnp.mean(vf, axis=-1, keepdims=True)
    var = jnp.mean(jnp.square(vf - mu), axis=-1, keepdims=True)
    v = ((vf - mu) * lax.rsqrt(var + LN_EPS) * ln_g.astype(jnp.float32) + ln_b.astype(jnp.float32)).astype(p.dtype)
    bn, s, _ = v.shape
    v = v.reshape(bn, s // CHUNK, CHUNK, N_HEADS_A, HEAD_DIM)
    mask = jnp.tril(jnp.ones((CHUNK, CHUNK), dtype=bool))
    w = jnp.where(mask, w_s, 0.0)
    mixed = jnp.einsum('hts,bnshd->bnthd', w, v) + b_s.T[None, None, :, :, None]
    return u * mixed.reshape(bn, s, D_A)

def rg_lru_block(p, conv_w, conv_b, w_ra, b_ra, w_ix, b_ix, lam):
    xr, yg = jnp.split(p, 2, axis=-1)
    xr = causal_dwconv(xr, conv_w, conv_b)
    bn, s, _ = xr.shape
    xh = xr.reshape(bn, s, N_BLOCKS_B, HEAD_DIM)
    r = jax.nn.sigmoid(jnp.einsum('bshi,hij->bshj', xh, w_ra).reshape(bn, s, D_B) + b_ra)
    i = jax.nn.sigmoid(jnp.einsum('bshi,hij->bshj', xh, w_ix).reshape(bn, s, D_B) + b_ix)
    log_a = (-LRU_C * r.astype(jnp.float32)) * jax.nn.softplus(-lam.astype(jnp.float32))
    a = jnp.exp(log_a)
    bterm = jnp.sqrt(-jnp.expm1(2.0 * log_a)) * (i * xr).astype(jnp.float32)

    def combine(left, right):
        a1, b1 = left
        a2, b2 = right
        return a1 * a2, a2 * b1 + b2

    _, h = lax.associative_scan(combine, (a, bterm), axis=1)
    return jax.nn.gelu(yg) * h.astype(p.dtype)

def rwkv7_time_mix(p, mu, w0, w2, a0, a2, g2, k_k, k_a, r_k, ln_w, ln_b):
    p = p + (token_shift(p) - p) * mu
    r, k, v, xw, xa, xg = jnp.split(
        p, [D_C, 2 * D_C, 3 * D_C, 3 * D_C + LORA_W, 3 * D_C + LORA_W + LORA_A], axis=-1)
    w = -jax.nn.softplus(-(w0 + jnp.tanh(xw) @ w2)) - 0.5
    decay = jnp.exp(-jnp.exp(w.astype(jnp.float32)))
    a = jax.nn.sigmoid(a0 + xa @ a2)
    g = jax.nn.sigmoid(xg) @ g2
    bn, s, _ = r.shape

    def heads(t):
        return t.astype(jnp.float32).reshape(bn, s, N_HEADS_C, HEAD_DIM)

    kk = heads(k * k_k)
    kk = kk * lax.rsqrt(jnp.maximum(jnp.sum(kk * kk, axis=-1, keepdims=True), 1e-24))
    k = k * (1.0 + (a - 1.0) * k_a)
    rh, kh, vh, wh, ah = heads(r), heads(k), heads(v), heads(decay), heads(a)

    def step(state, inp):
        r_t, w_t, k_t, v_t, kk_t, a_t = inp
        sa = jnp.einsum('bhvk,bhk->bhv', state, kk_t)
        state = (state * w_t[:, :, None, :]
                 - sa[..., :, None] * (kk_t * a_t)[..., None, :]
                 + v_t[..., :, None] * k_t[..., None, :])
        return state, jnp.einsum('bhvk,bhk->bhv', state, r_t)

    seq_first = [jnp.moveaxis(t, 1, 0) for t in (rh, wh, kh, vh, kk, ah)]
    state0 = jnp.zeros((bn, N_HEADS_C, HEAD_DIM, HEAD_DIM), jnp.float32)
    _, out = lax.scan(step, state0, tuple(seq_first))
    out = jnp.moveaxis(out, 0, 1)
    mean = jnp.mean(out, axis=-1, keepdims=True)
    var = jnp.mean(jnp.square(out - mean), axis=-1, keepdims=True)
    out = ((out - mean) * lax.rsqrt(var + GN_EPS) * ln_w.astype(jnp.float32).reshape(N_HEADS_C, HEAD_DIM)
           + ln_b.astype(jnp.float32).reshape(N_HEADS_C, HEAD_DIM))
    bonus = jnp.sum(rh * kh * r_k.astype(jnp.float32), axis=-1, keepdims=True) * vh
    out = (out + bonus).reshape(bn, s, D_C).astype(p.dtype)
    return out * g

def conv_glu_ffn(h, w_up, conv_w, conv_b, w_down):
    gate, val = jnp.split(h @ w_up, 2, axis=-1)
    gate = causal_dwconv(gate, conv_w, conv_b)
    return (jax.nn.silu(gate) * val) @ w_down

def first_inputs(seed: int = 0) -> dict:
    key = jax.random.key(seed)
    ks = jax.random.split(key, 40)
    f32 = jnp.float32
    nrm = lambda k, shape, s: jax.random.normal(k, shape, f32) * s
    L = DEPTH
    u_a = jax.random.uniform(ks[15], (L, D_B), f32, 0.9, 0.999)
    s_a = u_a ** (1.0 / LRU_C)
    return {
        "x": nrm(ks[0], (BATCH, SEQ, D_MODEL), 1.0),
        "c": nrm(ks[1], (BATCH, D_MODEL), 1.0),
        "w_mod": nrm(ks[2], (L, D_MODEL, N_MOD * D_MODEL), 0.5 * D_MODEL ** -0.5),
        "b_mod": nrm(ks[3], (L, N_MOD * D_MODEL), 0.02),
        "norm_mix": 1.0 + nrm(ks[4], (L, D_MODEL), 0.02),
        "w_in": nrm(ks[5], (L, D_MODEL, P_IN), D_MODEL ** -0.5),
        "w_out": nrm(ks[6], (L, D_MIX, D_MODEL), D_MIX ** -0.5),
        "sgu_ln_g": 1.0 + nrm(ks[7], (L, D_A), 0.02),
        "sgu_ln_b": nrm(ks[8], (L, D_A), 0.02),
        "sgu_w": nrm(ks[9], (L, N_HEADS_A, CHUNK, CHUNK), 0.05),
        "sgu_b": 1.0 + nrm(ks[10], (L, N_HEADS_A, CHUNK), 0.02),
        "lru_conv_w": nrm(ks[11], (L, CONV_B, D_B), CONV_B ** -0.5),
        "lru_conv_b": nrm(ks[12], (L, D_B), 0.02),
        "lru_w_a": nrm(ks[13], (L, N_BLOCKS_B, HEAD_DIM, HEAD_DIM), HEAD_DIM ** -0.5),
        "lru_b_a": nrm(ks[14], (L, D_B), 0.02),
        "lru_w_x": nrm(ks[16], (L, N_BLOCKS_B, HEAD_DIM, HEAD_DIM), HEAD_DIM ** -0.5),
        "lru_b_x": nrm(ks[17], (L, D_B), 0.02),
        "lru_lambda": jnp.log(s_a) - jnp.log1p(-s_a),
        "rwkv_mu": jax.random.uniform(ks[18], (L, P_C), f32, 0.0, 1.0),
        "rwkv_w0": jax.random.uniform(ks[19], (L, D_C), f32, -6.0, -1.0),
        "rwkv_w2": nrm(ks[20], (L, LORA_W, D_C), 0.5 * LORA_W ** -0.5),
        "rwkv_a0": nrm(ks[21], (L, D_C), 0.1),
        "rwkv_a2": nrm(ks[22], (L, LORA_A, D_C), 0.5 * LORA_A ** -0.5),
        "rwkv_g2": nrm(ks[23], (L, LORA_G, D_C), LORA_G ** -0.5),
        "rwkv_k_k": 0.85 + nrm(ks[24], (L, D_C), 0.02),
        "rwkv_k_a": 1.0 + nrm(ks[25], (L, D_C), 0.02),
        "rwkv_r_k": nrm(ks[26], (L, N_HEADS_C, HEAD_DIM), 0.1),
        "rwkv_ln_w": 1.0 + nrm(ks[27], (L, D_C), 0.02),
        "rwkv_ln_b": nrm(ks[28], (L, D_C), 0.02),
        "norm_ffn": 1.0 + nrm(ks[29], (L, D_MODEL), 0.02),
        "ffn_w_up": nrm(ks[30], (L, D_MODEL, 2 * D_FF), D_MODEL ** -0.5),
        "ffn_conv_w": nrm(ks[31], (L, CONV_FF, D_FF), CONV_FF ** -0.5),
        "ffn_conv_b": nrm(ks[32], (L, D_FF), 0.02),
        "ffn_w_down": nrm(ks[33], (L, D_FF, D_MODEL), D_FF ** -0.5),
        "norm_final": 1.0 + nrm(ks[34], (D_MODEL,), 0.02),
    }

def first_block(x, c, w_mod, b_mod, norm_mix, w_in, w_out,
              sgu_ln_g, sgu_ln_b, sgu_w, sgu_b,
              lru_conv_w, lru_conv_b, lru_w_a, lru_b_a, lru_w_x, lru_b_x, lru_lambda,
              rwkv_mu, rwkv_w0, rwkv_w2, rwkv_a0, rwkv_a2, rwkv_g2, rwkv_k_k, rwkv_k_a,
              rwkv_r_k, rwkv_ln_w, rwkv_ln_b,
              norm_ffn, ffn_w_up, ffn_conv_w, ffn_conv_b, ffn_w_down, norm_final):
    c_act = jax.nn.silu(c)
    for l in range(DEPTH):
        mod = c_act @ w_mod[l] + b_mod[l]
        sh1, sc1, gt1, sh2, sc2, gt2 = [m[:, None, :] for m in jnp.split(mod, N_MOD, axis=-1)]
        h = rms_norm(x, norm_mix[l]) * (1.0 + sc1) + sh1
        p = h @ w_in[l]
        p_a, p_b, p_c = jnp.split(p, [P_A, P_A + P_B], axis=-1)
        y_a = chunked_sgu(p_a, sgu_ln_g[l], sgu_ln_b[l], sgu_w[l], sgu_b[l])
        y_b = rg_lru_block(p_b, lru_conv_w[l], lru_conv_b[l], lru_w_a[l], lru_b_a[l],
                           lru_w_x[l], lru_b_x[l], lru_lambda[l])
        y_c = rwkv7_time_mix(p_c, rwkv_mu[l], rwkv_w0[l], rwkv_w2[l], rwkv_a0[l], rwkv_a2[l],
                             rwkv_g2[l], rwkv_k_k[l], rwkv_k_a[l], rwkv_r_k[l],
                             rwkv_ln_w[l], rwkv_ln_b[l])
        y = jnp.concatenate([y_a, y_b, y_c], axis=-1) @ w_out[l]
        x = x + gt1 * y
        h = rms_norm(x, norm_ffn[l]) * (1.0 + sc2) + sh2
        x = x + gt2 * conv_glu_ffn(h, ffn_w_up[l], ffn_conv_w[l], ffn_conv_b[l], ffn_w_down[l])
    return rms_norm(x, norm_final)


_first_inputs = first_inputs


def first_inputs(seed=0):
    import zlib

    import numpy as np

    out = dict(_first_inputs(seed))
    spreads = {}
    factors = {'norm_mix': 8.0,
     'sgu_ln_g': 64.0,
     'sgu_ln_b': 64.0,
     'sgu_b': 64.0,
     'lru_conv_b': 34.712,
     'lru_b_a': 64.0,
     'lru_b_x': 64.0,
     'rwkv_w2': 64.0,
     'rwkv_a0': 8.0,
     'rwkv_k_k': 64.0,
     'rwkv_k_a': 8.0,
     'rwkv_ln_w': 64.0,
     'rwkv_ln_b': 64.0,
     'norm_ffn': 64.0,
     'ffn_conv_b': 64.0,
     'norm_final': 7.89,
     'rwkv_w0': 8.0}
    for name, (base, spread) in spreads.items():
        noise = np.random.default_rng([zlib.crc32(name.encode()), seed]).standard_normal(out[name].shape)
        drawn = base * np.exp(spread * noise) if base else spread * noise
        out[name] = __import__('jax').numpy.asarray(drawn.astype(out[name].dtype))
    for name, factor in factors.items():
        out[name] = (out[name] * factor).astype(out[name].dtype)
    return out


_narrow_inputs = first_inputs


def first_inputs(seed=0):

    out = dict(_narrow_inputs(seed))
    wider = {'sgu_ln_g': 12.0,
     'sgu_ln_b': 12.0,
     'sgu_b': 4.91,
     'lru_b_a': 5.84,
     'lru_b_x': 5.64,
     'rwkv_k_k': 12.0,
     'rwkv_ln_w': 12.0,
     'rwkv_ln_b': 12.0,
     'ffn_conv_b': 3.14,
     'norm_final': 3.17}
    for name, times in wider.items():
        mean = out[name].mean()
        out[name] = (mean + times * (out[name] - mean)).astype(out[name].dtype)
    return out


CHUNK_2 = 64
D_MIX_2 = D_MODEL
S5_WIDTH = D_MIX_2 // 2
S5_GROUP = 16
S5_GROUPS = S5_WIDTH // S5_GROUP
S5_STATE = 64
S5_DT_MIN = 0.001
S5_DT_MAX = 0.1
RET_WIDTH = D_MIX_2 - S5_WIDTH
RET_HEADS = 4
RET_DV = RET_WIDTH // RET_HEADS
RET_DK = RET_DV // 2
D_IN = S5_WIDTH + 2 * RET_HEADS * RET_DK + 2 * RET_WIDTH
CONV_W = 3
ROPE_BASE = 10000.0
DEEPNORM_ALPHA = (2.0 * DEPTH) ** 0.25
DEEPNORM_BETA = (8.0 * DEPTH) ** -0.25


def layer_norm(x, g, b):
    x32 = x.astype(jnp.float32)
    mu = jnp.mean(x32, axis=-1, keepdims=True)
    xc = x32 - mu
    var = jnp.mean(jnp.square(xc), axis=-1, keepdims=True)
    y = xc * lax.rsqrt(var + LN_EPS) * g.astype(jnp.float32) + b.astype(jnp.float32)
    return y.astype(x.dtype)

def rms_norm_2(x, g):
    x32 = x.astype(jnp.float32)
    y = x32 * lax.rsqrt(jnp.mean(jnp.square(x32), axis=-1, keepdims=True) + LN_EPS)
    return y * g.astype(jnp.float32)

def rotary(x, pos):
    half = x.shape[-1] // 2
    freqs = ROPE_BASE ** (-jnp.arange(half, dtype=jnp.float32) / half)
    ang = pos[:, None] * freqs[None, :]
    cos = jnp.cos(ang)[None, :, None, :]
    sin = jnp.sin(ang)[None, :, None, :]
    x1, x2 = x[..., :half], x[..., half:]
    return jnp.concatenate([x1 * cos - x2 * sin, x1 * sin + x2 * cos], axis=-1)

def _ssm_combine(left, right):
    a_l, b_l = left
    a_r, b_r = right
    return a_r * a_l, a_r * b_l + b_r

def s5_mixer(u, lam_re, lam_im, b_re, b_im, c_re, c_im, d, log_step, glu_w, glu_b):
    bsz, seq_len, _ = u.shape
    f32 = jnp.float32
    u32 = u.astype(f32).reshape(bsz, seq_len, S5_GROUPS, S5_GROUP)
    lam = lax.complex(lam_re.astype(f32), lam_im.astype(f32))
    dt = jnp.exp(log_step.astype(f32))[:, None]
    lam_bar = jnp.exp(lam * dt)
    b = lax.complex(b_re.astype(f32), b_im.astype(f32))
    b_bar = ((lam_bar - 1.0) / lam)[..., None] * b
    bu = jnp.einsum('blgc,gpc->blgp', u32.astype(jnp.complex64), b_bar)
    a_elems = jnp.broadcast_to(lam_bar[None, None], (1, seq_len, S5_GROUPS, S5_STATE))
    _, states = lax.associative_scan(_ssm_combine, (a_elems, bu), axis=1)
    c = lax.complex(c_re.astype(f32), c_im.astype(f32))
    y = jnp.real(jnp.einsum('blgp,gcp->blgc', states, c))
    y = y + d.astype(f32).reshape(S5_GROUPS, S5_GROUP) * u32
    y = jax.nn.gelu(y.reshape(bsz, seq_len, S5_WIDTH))
    return y * jax.nn.sigmoid(y @ glu_w.astype(f32) + glu_b.astype(f32))

def retention(q, k, v, gn_gain):
    bsz, seq_len = q.shape[0], q.shape[1]
    n_chunks = seq_len // CHUNK_2
    f32 = jnp.float32
    log_gamma = jnp.log1p(-(2.0 ** (-5.0 - jnp.arange(RET_HEADS, dtype=f32))))
    k = k * (RET_DK ** -0.5)
    qc = q.reshape(bsz, n_chunks, CHUNK_2, RET_HEADS, RET_DK)
    kc = k.reshape(bsz, n_chunks, CHUNK_2, RET_HEADS, RET_DK)
    vc = v.reshape(bsz, n_chunks, CHUNK_2, RET_HEADS, RET_DV)
    pos = jnp.arange(CHUNK_2, dtype=f32)
    intra_decay = jnp.exp(jnp.abs(pos[:, None] - pos[None, :])[None] * log_gamma[:, None, None])
    scores = jnp.einsum('bncht,bnmht->bhncm', qc, kc) * intra_decay[:, None]
    intra = jnp.einsum('bhncm,bnmhe->bnche', scores, vc)
    zeta = jnp.exp((CHUNK_2 - 1.0 - pos)[None, :] * log_gamma[:, None])
    xi = jnp.exp((pos + 1.0)[None, :] * log_gamma[:, None])
    kv = jnp.einsum('bnmht,hm,bnmhe->nbhte', kc, zeta, vc)
    chunk_decay = jnp.exp(CHUNK_2 * log_gamma)[:, None, None]

    def step(state, kv_n):
        return state * chunk_decay + kv_n, state

    init = jnp.zeros((bsz, RET_HEADS, RET_DK, RET_DV), f32)
    _, states_before = lax.scan(step, init, kv)
    cross = jnp.einsum('bncht,hc,nbhte->bnche', qc, xi, states_before)
    out = intra + cross
    mu = jnp.mean(out, axis=-1, keepdims=True)
    var = jnp.mean(jnp.square(out - mu), axis=-1, keepdims=True)
    out = (out - mu) * lax.rsqrt(var + LN_EPS) * gn_gain.astype(f32).reshape(RET_HEADS, RET_DV)
    return out.reshape(bsz, seq_len, RET_WIDTH)

def hybrid_mixer(x, w_in, lam_re, lam_im, b_re, b_im, c_re, c_im, d, log_step,
                 glu_w, glu_b, s5_gain, gn_gain, w_out):
    bsz, seq_len, _ = x.shape
    h = x @ w_in
    o1 = S5_WIDTH
    o2 = o1 + RET_HEADS * RET_DK
    o3 = o2 + RET_HEADS * RET_DK
    o4 = o3 + RET_WIDTH
    u_s5 = h[..., :o1]
    pos = jnp.arange(seq_len, dtype=jnp.float32)
    q = rotary(h[..., o1:o2].astype(jnp.float32).reshape(bsz, seq_len, RET_HEADS, RET_DK), pos)
    k = rotary(h[..., o2:o3].astype(jnp.float32).reshape(bsz, seq_len, RET_HEADS, RET_DK), pos)
    v = h[..., o3:o4].astype(jnp.float32).reshape(bsz, seq_len, RET_HEADS, RET_DV)
    gate = h[..., o4:].astype(jnp.float32)
    y_s5 = rms_norm_2(s5_mixer(u_s5, lam_re, lam_im, b_re, b_im, c_re, c_im, d, log_step, glu_w, glu_b), s5_gain)
    y_ret = retention(q, k, v, gn_gain) * jax.nn.silu(gate)
    y = jnp.concatenate([y_s5, y_ret], axis=-1).astype(x.dtype)
    return y @ w_out

def conv_ffn(x, w_up, conv_w, conv_b, w_down):
    seq_len = x.shape[1]
    ug = x @ w_up
    a, g = ug[..., :D_FF], ug[..., D_FF:]
    a_pad = jnp.pad(a, ((0, 0), (CONV_W - 1, 0), (0, 0)))
    a = sum(conv_w[i] * a_pad[:, i:i + seq_len] for i in range(CONV_W)) + conv_b
    return (jax.nn.silu(a) * g) @ w_down

def second_inputs(seed: int = 0) -> dict:
    key = jax.random.key(seed)
    ks = jax.random.split(key, 24)
    f32 = jnp.float32
    nrm = lambda k, shape, s: jax.random.normal(k, shape, f32) * s
    x = jax.random.normal(ks[0], (BATCH, SEQ, D_MODEL), f32)
    col_scale = jnp.concatenate([
        jnp.ones((S5_WIDTH + 2 * RET_HEADS * RET_DK,), f32),
        jnp.full((RET_WIDTH,), DEEPNORM_BETA, f32),
        jnp.ones((RET_WIDTH,), f32)])
    w_in = nrm(ks[1], (DEPTH, D_MODEL, D_IN), D_MODEL ** -0.5) * col_scale
    s5_lambda_re = -0.5 + nrm(ks[2], (DEPTH, S5_GROUPS, S5_STATE), 0.01)
    s5_lambda_im = math.pi * jnp.arange(S5_STATE, dtype=f32)[None, None, :] + nrm(ks[3], (DEPTH, S5_GROUPS, S5_STATE), 0.01)
    s5_b_re = nrm(ks[4], (DEPTH, S5_GROUPS, S5_STATE, S5_GROUP), (2.0 * S5_GROUP) ** -0.5)
    s5_b_im = nrm(ks[5], (DEPTH, S5_GROUPS, S5_STATE, S5_GROUP), (2.0 * S5_GROUP) ** -0.5)
    s5_c_re = nrm(ks[6], (DEPTH, S5_GROUPS, S5_GROUP, S5_STATE), (2.0 * S5_STATE) ** -0.5)
    s5_c_im = nrm(ks[7], (DEPTH, S5_GROUPS, S5_GROUP, S5_STATE), (2.0 * S5_STATE) ** -0.5)
    s5_d = nrm(ks[8], (DEPTH, S5_WIDTH), 1.0)
    s5_log_step = jax.random.uniform(ks[9], (DEPTH, S5_GROUPS), f32, math.log(S5_DT_MIN), math.log(S5_DT_MAX))
    s5_glu_w = nrm(ks[10], (DEPTH, S5_WIDTH, S5_WIDTH), S5_WIDTH ** -0.5)
    s5_glu_b = nrm(ks[11], (DEPTH, S5_WIDTH), 0.01)
    s5_out_gain = 1.0 + nrm(ks[12], (DEPTH, S5_WIDTH), 0.01)
    ret_gn_gain = 1.0 + nrm(ks[13], (DEPTH, RET_WIDTH), 0.01)
    w_out = nrm(ks[14], (DEPTH, D_MIX_2, D_MODEL), D_MIX_2 ** -0.5 * DEEPNORM_BETA)
    ln1_g = 1.0 + nrm(ks[15], (DEPTH, D_MODEL), 0.01)
    ln1_b = nrm(ks[16], (DEPTH, D_MODEL), 0.01)
    ffn_w_up = nrm(ks[17], (DEPTH, D_MODEL, 2 * D_FF), D_MODEL ** -0.5)
    ffn_conv_w = nrm(ks[18], (DEPTH, CONV_W, D_FF), CONV_W ** -0.5)
    ffn_conv_b = nrm(ks[19], (DEPTH, D_FF), 0.01)
    ffn_w_down = nrm(ks[20], (DEPTH, D_FF, D_MODEL), D_FF ** -0.5 * DEEPNORM_BETA)
    ln2_g = 1.0 + nrm(ks[21], (DEPTH, D_MODEL), 0.01)
    ln2_b = nrm(ks[22], (DEPTH, D_MODEL), 0.01)
    return {"x": x, "w_in": w_in, "s5_lambda_re": s5_lambda_re, "s5_lambda_im": s5_lambda_im,
            "s5_b_re": s5_b_re, "s5_b_im": s5_b_im, "s5_c_re": s5_c_re, "s5_c_im": s5_c_im,
            "s5_d": s5_d, "s5_log_step": s5_log_step, "s5_glu_w": s5_glu_w, "s5_glu_b": s5_glu_b,
            "s5_out_gain": s5_out_gain, "ret_gn_gain": ret_gn_gain, "w_out": w_out,
            "ln1_g": ln1_g, "ln1_b": ln1_b, "ffn_w_up": ffn_w_up, "ffn_conv_w": ffn_conv_w,
            "ffn_conv_b": ffn_conv_b, "ffn_w_down": ffn_w_down, "ln2_g": ln2_g, "ln2_b": ln2_b}

def second_block(x, w_in, s5_lambda_re, s5_lambda_im, s5_b_re, s5_b_im, s5_c_re, s5_c_im,
              s5_d, s5_log_step, s5_glu_w, s5_glu_b, s5_out_gain, ret_gn_gain, w_out,
              ln1_g, ln1_b, ffn_w_up, ffn_conv_w, ffn_conv_b, ffn_w_down, ln2_g, ln2_b):
    for l in range(DEPTH):
        mix = hybrid_mixer(x, w_in[l], s5_lambda_re[l], s5_lambda_im[l], s5_b_re[l], s5_b_im[l],
                           s5_c_re[l], s5_c_im[l], s5_d[l], s5_log_step[l], s5_glu_w[l], s5_glu_b[l],
                           s5_out_gain[l], ret_gn_gain[l], w_out[l])
        x = layer_norm(DEEPNORM_ALPHA * x + mix, ln1_g[l], ln1_b[l])
        ffn = conv_ffn(x, ffn_w_up[l], ffn_conv_w[l], ffn_conv_b[l], ffn_w_down[l])
        x = layer_norm(DEEPNORM_ALPHA * x + ffn, ln2_g[l], ln2_b[l])
    return x


_first_inputs_2 = second_inputs


def second_inputs(seed=0):
    import zlib

    import numpy as np

    out = dict(_first_inputs_2(seed))
    spreads = {}
    factors = {'s5_lambda_re': 8.0,
     's5_b_re': 3.564,
     's5_b_im': 3.608,
     's5_c_re': 3.612,
     's5_c_im': 3.612,
     's5_glu_b': 8.0,
     's5_out_gain': 8.0,
     'ret_gn_gain': 8.0,
     'ln1_g': 5.488,
     'ln1_b': 5.496,
     'ffn_conv_b': 8.0,
     'ln2_g': 5.49,
     'ln2_b': 5.652}
    for name, (base, spread) in spreads.items():
        noise = np.random.default_rng([zlib.crc32(name.encode()), seed]).standard_normal(out[name].shape)
        drawn = base * np.exp(spread * noise) if base else spread * noise
        out[name] = __import__('jax').numpy.asarray(drawn.astype(out[name].dtype))
    for name, factor in factors.items():
        out[name] = (out[name] * factor).astype(out[name].dtype)
    return out


_narrow_inputs_2 = second_inputs


def second_inputs(seed=0):

    out = dict(_narrow_inputs_2(seed))
    wider = {'s5_lambda_re': 12.0,
     's5_out_gain': 5.57,
     'ret_gn_gain': 9.78,
     'ln1_g': 4.76,
     'ln1_b': 4.81,
     'ffn_conv_b': 5.0,
     'ln2_g': 6.18,
     'ln2_b': 6.18}
    for name, times in wider.items():
        mean = out[name].mean()
        out[name] = (mean + times * (out[name] - mean)).astype(out[name].dtype)
    return out


def setup_inputs(seed=0):
    out = dict(first_inputs(seed))
    for name, value in second_inputs(seed + 1).items():
        if name != "x":
            out[name + "_2"] = value
    return out


def reference(
    x, c, w_mod, b_mod, norm_mix, w_in, w_out, sgu_ln_g, sgu_ln_b, sgu_w, sgu_b, lru_conv_w,
    lru_conv_b, lru_w_a, lru_b_a, lru_w_x, lru_b_x, lru_lambda, rwkv_mu, rwkv_w0, rwkv_w2,
    rwkv_a0, rwkv_a2, rwkv_g2, rwkv_k_k, rwkv_k_a, rwkv_r_k, rwkv_ln_w, rwkv_ln_b, norm_ffn,
    ffn_w_up, ffn_conv_w, ffn_conv_b, ffn_w_down, norm_final, w_in_2, s5_lambda_re_2,
    s5_lambda_im_2, s5_b_re_2, s5_b_im_2, s5_c_re_2, s5_c_im_2, s5_d_2, s5_log_step_2,
    s5_glu_w_2, s5_glu_b_2, s5_out_gain_2, ret_gn_gain_2, w_out_2, ln1_g_2, ln1_b_2, ffn_w_up_2,
    ffn_conv_w_2, ffn_conv_b_2, ffn_w_down_2, ln2_g_2, ln2_b_2,
):
    x = first_block(
        x, c, w_mod, b_mod, norm_mix, w_in, w_out, sgu_ln_g, sgu_ln_b, sgu_w, sgu_b, lru_conv_w,
        lru_conv_b, lru_w_a, lru_b_a, lru_w_x, lru_b_x, lru_lambda, rwkv_mu, rwkv_w0, rwkv_w2,
        rwkv_a0, rwkv_a2, rwkv_g2, rwkv_k_k, rwkv_k_a, rwkv_r_k, rwkv_ln_w, rwkv_ln_b, norm_ffn,
        ffn_w_up, ffn_conv_w, ffn_conv_b, ffn_w_down, norm_final,
    )
    return second_block(
        x, w_in_2, s5_lambda_re_2, s5_lambda_im_2, s5_b_re_2, s5_b_im_2, s5_c_re_2, s5_c_im_2,
        s5_d_2, s5_log_step_2, s5_glu_w_2, s5_glu_b_2, s5_out_gain_2, ret_gn_gain_2, w_out_2,
        ln1_g_2, ln1_b_2, ffn_w_up_2, ffn_conv_w_2, ffn_conv_b_2, ffn_w_down_2, ln2_g_2,
        ln2_b_2,
    )


_drawn_inputs = setup_inputs


def setup_inputs(seed=0):
    import zlib

    import numpy as np

    out = dict(_drawn_inputs(seed))
    spreads = {}
    factors = {'rwkv_k_k': 2.694, 's5_lambda_re_2': 3.237, 's5_glu_b_2': 8.0, 's5_out_gain_2': 4.303}
    for name, (base, spread) in spreads.items():
        noise = np.random.default_rng([zlib.crc32(name.encode()), seed]).standard_normal(out[name].shape)
        drawn = base * np.exp(spread * noise) if base else spread * noise
        out[name] = __import__('jax').numpy.asarray(drawn.astype(out[name].dtype))
    for name, factor in factors.items():
        out[name] = (out[name] * factor).astype(out[name].dtype)
    return out
```

```python
from contextlib import ExitStack

import numpy as np
import concourse.bass as bass
from concourse import mybir

F32 = mybir.dt.float32
BF16 = mybir.dt.bfloat16
F32R = mybir.dt.float32r
I32 = mybir.dt.int32
ALU = mybir.AluOpType
ACT = mybir.ActivationFunctionType

P = 128
D = 1024
S = 1024
DT = D // P
FF = 2816
FT = FF // P
HD = 64
EPS = 1e-6
LN_EPS = 1e-5
GN_EPS = 64e-5
LRU_C = 8.0
ALPHA = 2.0 ** 0.25
CH = 128
NC = S // CH
S5_T = 8
S5_G = 32
S5_N = S // S5_T
RND = 12582912.0

VECTORS = [
    ("norm_mix", 8), ("b_mod", 48), ("lru_conv_w", 12), ("lru_conv_b", 3), ("lru_b_a", 3), ("lru_b_x", 3),
    ("lru_lambda", 3), ("rwkv_mu", 11), ("rwkv_w0", 3), ("rwkv_a0", 3), ("rwkv_k_k", 3), ("rwkv_k_a", 3),
    ("rwkv_r_k", 3), ("rwkv_ln_w", 3), ("rwkv_ln_b", 3), ("norm_ffn", 8), ("ffn_conv_w", 66), ("ffn_conv_b", 22),
    ("norm_final", 8), ("s5_d_2", 4), ("s5_glu_b_2", 4), ("s5_out_gain_2", 4), ("ret_gn_gain_2", 4),
    ("ln1_g_2", 8), ("ln1_b_2", 8), ("ffn_conv_w_2", 66), ("ffn_conv_b_2", 22), ("ln2_g_2", 8), ("ln2_b_2", 8),
]
COL = {}
_at = 0
for _name, _n in VECTORS:
    COL[_name] = _at
    _at += _n
NVEC = _at

CONST = {}
_at = 0
for _name, _n in [("ident", 128), ("ones", 128), ("block_ones", 128), ("block_mean", 128), ("neg_m1", 128),
                  ("neg_m1t", 128), ("causal", 128)] + [(f"level{b}", 128) for b in (2, 4, 8, 16, 32, 64)] + [
                  ("swap_halves", 128), ("ret_zeta", 8), ("head0", 1),
                  ("head1", 1), ("sgn_re", 1), ("sgn_im", 1), ("ret_chunk", 2)]:
    CONST[_name] = (_at, _n)
    _at += _n
NCONST = _at
LEVELS = (2, 4, 8, 16, 32, 64)


def shape_constants():
    c = np.zeros((P, NCONST), np.float32)

    def put(name, a):
        at, n = CONST[name]
        c[:, at:at + n] = a

    r = np.arange(P)[:, None]
    k = np.arange(P)[None, :]
    put("ident", r == k)
    put("ones", 1.0)
    put("block_ones", r // HD == k // HD)
    put("block_mean", (r // HD == k // HD) / HD)
    m1 = (r % 2 == 1) & (k == r - 1)
    put("neg_m1", -1.0 * m1)
    put("neg_m1t", -1.0 * m1.T)
    put("causal", r <= k)
    for b in LEVELS:
        put(f"level{b}", (r // (2 * b) == k // (2 * b)) & ((r // b) % 2 == 1) & ((k // b) % 2 == 0))
    put("swap_halves", r == (k ^ 32))
    heads = np.arange(4, dtype=np.float64)
    lg = np.log1p(-(2.0 ** (-5.0 - heads)))
    same = (r // 64) == (k // 64)
    decay = (np.concatenate([np.where(same, np.exp(np.abs(r - k) * g), 0.0) * 64.0 ** -0.5 for g in lg], 1))
    tcol = np.arange(P)
    xi = np.concatenate([np.exp(((tcol % 64)[None, :] + 1.0) * lg[2 * i + tcol // 64][:, None]) for i in range(2)], 1)
    ret = np.concatenate([decay, xi], 1).astype(np.float32)
    put("ret_zeta", np.stack([np.where(tcol // 64 == j, np.exp((63.0 - (tcol % 64)) * x) * 64.0 ** -0.5, 0.0)
                              for j in range(2) for x in lg], 1))
    put("head0", (r < 64))
    put("head1", (r >= 64))
    put("sgn_re", np.where(r < 64, -1.0, 1.0))
    put("sgn_im", np.where(r < 64, 1.0, -1.0))
    put("ret_chunk", np.stack([np.exp(64 * lg[2 * i + tcol // 64]) for i in range(2)], 1))
    keep = np.concatenate([r < k, r <= k, r < k, r <= k], 1).astype(np.int32)
    half = 32
    freqs = np.float32(10000.0) ** (-np.arange(half, dtype=np.float32) / np.float32(half))
    ang = (np.arange(S, dtype=np.float32)[None, :] * freqs.astype(np.float32)[:, None]).astype(np.float64)
    cos, sin = np.cos(ang), np.sin(ang)
    rope = np.stack([np.concatenate([cos] * 4, 0), np.concatenate([-sin, sin] * 2, 0)], 1).astype(np.float32)
    n_row = np.broadcast_to(np.arange(S5_N, dtype=np.float32), (P, S5_N)).copy()
    return {"const": c, "keep": keep, "ret": ret, "rope": rope, "n_row": n_row}


def build(nc, a):
    with ExitStack() as ctx:
        sems, counts = {}, {}

        def E(name):
            if name not in sems:
                sems[name] = ctx.enter_context(nc.semaphore(name))
            return sems[name]

        def sb(name, shape, dt=F32):
            return ctx.enter_context(nc.sbuf_tensor(name, shape, dt))

        with nc.sbuf_tensor("work", [P, 47, S], F32) as W:
            pass
        sb("slots_0_7", [P, 8, S])
        HR = sb("rhs_rounded", [P, 8, S], F32R)
        sb("slots_16_43", [P, 28, S])
        WR = sb("weights_rounded", [P, 2, S], F32R)
        sb("slot_46", [P, S])
        slot_47 = sb("slot_47", [P, S])
        par = sb("par", [P, NVEC])
        cst = sb("cst", [P, NCONST])
        sm = sb("small", [P, 320])
        bs = sb("sgu_bias", [P, 2, P])
        keep = sb("keep", [P, 512], I32)
        flat42 = W[:, 42:44, :].rearrange("p a n -> p (a n)")
        lora_w = flat42[:, 0:1152].rearrange("p (g n) -> p g n", g=3)
        lru_w = flat42[:, 1152:1920].rearrange("p (g i n) -> p g i n", g=2, i=3)
        PT = [ctx.enter_context(nc.psum_tensor(f"pt{i}", [P, S], F32)) for i in range(4)]

        def w(slot):
            return W[:, slot, :] if slot < 47 else slot_47[:, :]

        def col(name, i=0, n=1):
            return par[:, COL[name] + i:COL[name] + i + n]

        def const(name):
            at, n = CONST[name]
            return cst[:, at:at + n]

        def small(at, n=1):
            return sm[:, at:at + n]

        def bank(b):
            return PT[b // 2][:, (b % 2) * 512:(b % 2) * 512 + 512]

        MOD, G1, G2, OMM, CLRU, NCLRU, OMKA, EPSC, PMID, PEND, STAT = 0, 48, 56, 64, 76, 80, 84, 88, 92, 116, 140

        X, H = 0, 8
        U, V, XR, G, T, RR, KK, VV = 16, 18, 20, 23, 26, 29, 32, 35
        RING = 38
        NRING = 4
        MODRING = 44
        XWA, XG, RSTD, CB = 46, 47, 47, 37
        Z, B, GG, BV = 8, 11, (14, 15, 18), 19
        T1, T2, T3, T4, T5 = 22, 26, 27, 28, 44
        CA, CB_, CC, CD = (22, 26, 27), (28, 46, 47), (40, 42, 43), (44, 45, 41)
        Y1 = (16, 17, 23, 24, 25, 11, 12, 13)

        plan, place, ordinal = [], {}, {}
        n_by = {"act": 0, "dve": 0}

        def use(name, eng):
            n_by[eng] += 1
            place[name] = len(plan)
            ordinal[name] = n_by[eng]
            plan.append((name, eng))

        def pt(name):
            return PT[place[name] % 4]

        for nm, eng in [("ss1", "dve"), ("uA0", "act"), ("vA0", "act"), ("vA1", "act"), ("uA1", "act"),
                        ("xr0", "dve"), ("xr1", "dve"), ("xr2", "dve"),
                        ("mx00", "dve"), ("mx01", "dve"), ("mx10", "dve"), ("mx11", "dve")]:
            use(nm, eng)
        for i in range(3):
            use(f"yg{i}", "act")
            use(f"ra{i}", "act")
            use(f"ix{i}", "act")
        C_ORDER = (9, 10, 0, 1, 2, 3, 4, 5, 6, 7, 8)
        for j in C_ORDER:
            use(f"c{j}", "dve")
        for i in range(3):
            use(f"lw{i}", "act")
            use(f"la{i}", "act")
            use(f"lg{i}", "act")
            use(f"kks{i}", "dve")
            use(f"bon{i}", "dve")
        CORE_AT = len(plan)
        for i in range(3):
            use(f"gm{i}", "dve")
            use(f"gv{i}", "dve")
        for m in range(8):
            use(f"o{m}", "dve")
        use("ss2", "dve")
        use("ssf", "dve")
        PROJ2 = {"u0": 0, "u1": 1, "u2": 2, "u3": 3, "q0": 4, "q1": 5, "k0": 6, "k1": 7, "g0": 12, "g1": 13, "g2": 14, "g3": 15}
        S5_STEPS = {"A": (("br", "act"), ("brs", "act"), ("tp", "dve")), "B": (("xx", "dve"), ("xs", "dve")), "C": (("yy", "act"),)}
        ORDER2 = ["u0", "u1", "u2", "u3", "q0", "q1", ("A", 0), "k0", ("B", 0), "k1", "v0", ("C", 0), "v1", ("A", 1), "v2",
                  ("B", 1), "v3", ("C", 1), "g0", ("A", 2), ("B", 2), "g1", ("C", 2), "g2", ("A", 3), ("B", 3), "g3", ("C", 3)]
        for item in ORDER2:
            if isinstance(item, str):
                use("b2" + item, "act")
            else:
                for nm, eng in S5_STEPS[item[0]]:
                    use(f"{nm}{item[1]}", eng)
        for i in range(4):
            use(f"swap{i}", "dve")
        for m in range(4):
            use(f"glu{m}", "act")
        use("ss5", "dve")
        for i in range(2):
            use(f"kt{i}", "act")
        for i in range(2):
            for hh in range(2):
                use(f"sc{2 * i + hh}", "dve")
            use(f"kv{i}", "dve")
            for hh in range(2):
                use(f"ro{2 * i + hh}", "act")
        for h in range(4):
            use(f"rm{h}", "dve")
            use(f"rv{h}", "dve")
        for m in range(8):
            use(f"p{m}", "dve")
        use("lm1", "dve")
        use("lv1", "dve")
        use("lm2", "dve")
        use("lv2", "dve")

        def emptied_through(name):
            return {e: sum(1 for _, o in plan[:place[name] + 1] if o == e) for e in ("act", "dve")}

        counts_before = (emptied_through("ss2"), emptied_through("lv1"))

        def did(eng, ins, name):
            counts[name] = counts.get(name, 0) + 1
            ins.then_inc(E(name), 1)
            eng.wait_ge(E(name), counts[name])
            return counts[name]

        def filled(eng, name):
            eng.wait_ge(E("pt_filled"), place[name] + 1)

        def emptied(eng, ins, name, who):
            did(eng, ins, f"pt_emptied_{who}")

        def claim(pe, name):
            at = place[name] - 4
            if at >= 0:
                other, who = plan[at]
                pe.wait_ge(E(f"pt_emptied_{who}"), ordinal[other])

        ring = []

        def ring_use(name, src, slots):
            at = sum(n for _, _, n in ring)
            ring.append((name, src, slots))
            return at

        ring_at, ring_ord = {}, {}
        for name, src, n in [("uA0", a["w_in"][0], 1), ("vA", a["w_v"], 2)] + [
                (nm, a["w_in"][j], 1) for nm, j in
                [("uA1", 1)] + [(f"xr{i}", 4 + i) for i in range(3)] + [(f"yg{i}", 7 + i) for i in range(3)]
                + [(f"c{j}", 10 + j) for j in C_ORDER]]:
            ring_ord[name] = len(ring)
            ring_at[name] = ring_use(name, src, n)

        def wslot(name):
            return RING + ring_at[name] % NRING

        def ring_wait(pe, name):
            slot = ring_at[name] % NRING
            n = sum(1 for o, _, _ in ring[:ring_ord[name] + 1] if ring_at[o] % NRING == slot)
            pe.wait_ge(E(f"ring{slot}"), 16 * n)

        def stats_matmuls(pe, name, src, n, weights, ready, per=1):
            src = [src + k for k in range(n)] if isinstance(src, int) else src
            claim(pe, name)
            for k in range(n):
                if ready:
                    pe.wait_ge(E(ready[0]), ready[1] + per * (k + 1))
                for h in range(2):
                    ins = pe.matmul(pt(name)[:, h * 512:h * 512 + 512], weights, w(src[k])[:, h * 512:h * 512 + 512],
                                    start=(k == 0), stop=(k == n - 1), skip_group_check=True)
            ins.then_inc(E("pt_filled"), 1)

        def linear(pe, name, weights, rhs_slots, wait=None, ready=None):
            claim(pe, name)
            if wait:
                wait()
            n = len(rhs_slots)
            for h in range(2):
                for k, s in enumerate(rhs_slots):
                    if ready and h == 0:
                        pe.wait_ge(E(ready[0]), ready[1] + k + 1)
                    ins = pe.matmul(pt(name)[:, h * 512:h * 512 + 512], weights(k), w(s)[:, h * 512:h * 512 + 512],
                                    start=(k == 0), stop=(k == n - 1))
            ins.then_inc(E("pt_filled"), 1)

        def ring_weights(name):
            return lambda k: W[:, wslot(name), k * P:(k + 1) * P]

        def bank_x(i):
            return bank(i)

        def bank_t(i):
            return bank(3 + i)

        def scores(i, h):
            return w(CA[i])[:, h * 512:h * 512 + 512]

        def inverse(i):
            return w(CB_[i])[:, 0:512]

        def inv(i, h, transposed):
            return w(CB_[i])[:, h * 256 + transposed * P:h * 256 + transposed * P + P]

        def xbuf(i):
            return w(CB_[i])[:, 512:768]

        def rbuf(i):
            return w(CB_[i])[:, 768:896]

        def gbuf(i):
            return w(CB_[i])[:, 896:1024]

        def seqmaj(i):
            return w(CC[i])[:, 0:512].rearrange("p (x n) -> p x n", x=4)

        def vpad(i, h):
            return w(CC[i])[:, 512 + h * P:512 + h * P + P]

        def v_both(i):
            return w(CC[i])[:, 512:768].rearrange("p (a n) -> p a n", n=64)[:, 0:4:3, :]

        def s_scaled(i):
            return w(CC[i])[:, 768:896]

        def state(i):
            return w(CC[i])[:, 896:1024]

        def zupad(i, h, x):
            return w(CD[i])[:, h * 256 + x * P:h * 256 + x * P + P]

        def zu_both(i, x):
            return w(CD[i])[:, 0:512].rearrange("p (a n) -> p a n", n=64)[:, 2 * x:2 * x + 6:5, :]

        def bkpad(i, x, h):
            return w(CD[i])[:, 512 + x * 256 + h * P:512 + x * 256 + h * P + P]

        def both(base, i, step, tt):
            return W[:, base + i:base + i + step + 1:step, tt]

        def core_pool(pool):
            pool.wait_ge(E("pt_emptied_dve"), ordinal["bon2"])
            pool.wait_ge(E("p_end"), 3)
            for s in CA + CC + CD:
                did(pool, pool.memset(w(s), 0.0), "core_zeroed")
            for c in range(NC):
                tt = slice(c * CH, (c + 1) * CH)
                for i in range(3):
                    q = 3 * c + i
                    if c > 0:
                        pool.wait_ge(E("l_done"), q - 2)
                    for h in range(2):
                        rows = slice(64 * h, 64 * h + 64)
                        dst = w(CD[i])[rows, 512:1024].rearrange("p (x n) -> p x n", x=2)[:, :, h * P:h * P + P]
                        did(pool, pool.tensor_copy(dst, both(B, i, 21, tt)[rows]), "bk_padded")

        def core_act(act):
            act.wait_ge(E("core_zeroed"), 9)
            for c in range(NC):
                tt = slice(c * CH, (c + 1) * CH)
                for i in range(3):
                    q = 3 * c + i
                    act.wait_ge(E("transposed"), q + 1)
                    did(act, act.activation(w(CC[i])[:, 0:384], bank_x(i)[:, 0:384], ACT.Copy), "seq_major")
                    vdst = w(CC[i])[:, 512:768].rearrange("p (a n) -> p a n", n=64)[:, 0:4:3, :]
                    did(act, act.activation(vdst, bank_x(i)[:, 384:512].rearrange("p (a n) -> p a n", n=64), ACT.Copy),
                        "v_seq_major")
                for i in range(3):
                    act.wait_ge(E("mv_done"), 3 * c + i + 1)
                    did(act, act.activation(w(CC[i])[:, 384:512], bank_x(i)[:, 0:128], ACT.Copy), "mv_kept")
                for i in range(3):
                    act.wait_ge(E("zu_done"), 3 * c + i + 1)
                    for h in range(2):
                        dst = w(CD[i])[:, h * 256:h * 256 + 256].rearrange("p (x n) -> p x n", x=2)[:, :, h * 64:h * 64 + 64]
                        did(act, act.activation(dst, bank_t(i)[:, h * P:h * P + P].rearrange("p (x n) -> p x n", x=2),
                                                ACT.Copy, scale=-1.0), "zu_kept")
                for i in range(3):
                    act.wait_ge(E("chunk_done"), 3 * c + i + 1)
                    did(act, act.activation(w(Z + i)[:, tt], bank_t(i)[:, 0:128], ACT.Copy), "o_kept")

        def core_dve(dve):
            def V_(ins, name="dve_step"):
                return did(dve, ins, name)

            def heads(ap, n):
                return ap.rearrange("p (h n) -> p h n", h=2)

            def rep(m):
                return m.unsqueeze(1).to_broadcast([P, 2, P])

            dve.wait_ge(E("core_zeroed"), 9)
            dve.wait_ge(E("keep_in"), 16)
            for c in range(NC):
                tt = slice(c * CH, (c + 1) * CH)
                for h in range(2):
                    for i in range(3):
                        q = 3 * c + i
                        src = bank_t(i) if h == 0 else bank_x(i)
                        dve.wait_ge(E("products_done"), 6 * c + 3 * h + i + 1)
                        V_(dve.copy_predicated(scores(i, h), keep[:, :], src), "scores_kept")
                for i in range(3):
                    t4 = inverse(i).rearrange("p (h x n) -> p h x n", h=2, x=2)
                    V_(dve.tensor_tensor(t4[:, :, 1, :], w(CA[i]).rearrange("p (h n) -> p h n", h=2)[:, :, 0:128],
                                         rep(const("neg_m1t")), ALU.mult))
                    dve.wait_ge(E("l_done"), 3 * c + i + 1)
                    V_(dve.tensor_tensor(t4[:, :, 0, :], heads(bank_t(i)[:, 0:256], P), rep(const("neg_m1")), ALU.mult))
                    flat = inverse(i).rearrange("p (x n) -> p x n", x=4)
                    V_(dve.tensor_tensor(flat, flat, const("ident").unsqueeze(1).to_broadcast([P, 4, P]), ALU.add),
                       "inverse_ready")
                for n, b in enumerate(LEVELS):
                    for i in range(3):
                        dve.wait_ge(E("x_done"), (c * 6 + n) * 3 + i + 1)
                        V_(dve.tensor_tensor(heads(xbuf(i), P), heads(bank_x(i)[:, 0:256], P), rep(const(f"level{b}")),
                                             ALU.mult), "x_masked")
                    for i in range(3):
                        dve.wait_ge(E("t_done"), (c * 6 + n) * 3 + i + 1)
                        if n < 5:
                            V_(dve.tensor_tensor(inverse(i), inverse(i), bank_t(i), ALU.subtract), "inverse_ready")
                        else:
                            tt4 = inverse(i).rearrange("p (h x n) -> p h x n", h=2, x=2)[:, :, 1, :]
                            ps4 = bank_t(i).rearrange("p (h x n) -> p h x n", h=2, x=2)[:, :, 1, :]
                            V_(dve.tensor_tensor(tt4, tt4, ps4, ALU.subtract), "inverse_ready")
                for i in range(3):
                    V_(dve.tensor_scalar(s_scaled(i), state(i), small(PMID + 8 * i + c), None, ALU.mult), "state_scaled")
                for i in range(3):
                    dve.wait_ge(E("rg_done"), 3 * c + i + 1)
                    V_(dve.tensor_tensor(rbuf(i), bank_x(i)[:, 0:128], w(RR + i)[:, tt], ALU.add), "r_ready")
                    V_(dve.tensor_tensor(gbuf(i), bank_x(i)[:, 128:256], const("block_ones"), ALU.mult), "g_ready")
                for i in range(3):
                    dve.wait_ge(E("chunk_done"), 3 * c + i + 1)
                    V_(dve.scalar_tensor_tensor(state(i), bank_x(i)[:, 0:128], small(PEND + 8 * i + c),
                                                const("block_ones"), ALU.mult, ALU.mult), "state_new")

        def core_pe(pe):
            pe.wait_ge(E("pt_emptied_dve"), ordinal["bon2"])
            pe.wait_ge(E("core_zeroed"), 9)
            for c in range(NC):
                tt = slice(c * CH, (c + 1) * CH)
                for i in range(3):
                    if c > 0:
                        pe.wait_ge(E("state_new"), 3 * (c - 1) + i + 1)
                    for x, s in enumerate((Z + i, B + i, KK + i, VV + i)):
                        ins = pe.transpose(bank_x(i)[:, x * P:x * P + P], w(s)[:, tt], const("ident"))
                    ins.then_inc(E("transposed"), 1)
                for h in range(2):
                    for i in range(3):
                        q = 3 * c + i
                        dst = bank_t(i) if h == 0 else bank_x(i)
                        pe.wait_ge(E("bk_padded"), 2 * q + h + 1)
                        if h == 0 and c > 0:
                            pe.wait_ge(E("o_kept"), q - 2)
                        if h == 1:
                            pe.wait_ge(E("v_seq_major"), q + 1)
                        for x in range(2):
                            ins = pe.matmul(dst[:, x * 256:x * 256 + 256], bkpad(i, x, h), both(Z, i, 21, tt),
                                            start=True, stop=True, skip_group_check=True)
                        ins.then_inc(E("products_done"), 1)
                for i in range(3):
                    pe.wait_ge(E("scores_kept"), 6 * c + i + 1)
                    for h in range(2):
                        ins = pe.matmul(bank_t(i)[:, h * P:h * P + P], w(Z + i)[:, tt], bkpad(i, 0, h), start=True,
                                        stop=True, skip_group_check=True)
                    ins.then_inc(E("l_done"), 1)
                for n in range(6):
                    for i in range(3):
                        pe.wait_ge(E("inverse_ready"), c * 21 + 3 * n + i + 1)
                        for h in range(2):
                            ins = pe.matmul(bank_x(i)[:, h * P:h * P + P], scores(i, h)[:, 0:128], inv(i, h, 0),
                                            start=True, stop=True, skip_group_check=True)
                        ins.then_inc(E("x_done"), 1)
                    for i in range(3):
                        pe.wait_ge(E("x_masked"), (c * 6 + n) * 3 + i + 1)
                        for h in range(2):
                            xh = xbuf(i)[:, h * P:h * P + P]
                            if n < 5:
                                pe.matmul(bank_t(i)[:, h * 256:h * 256 + P], inv(i, h, 1), xh, start=True, stop=True,
                                          skip_group_check=True)
                            ins = pe.matmul(bank_t(i)[:, h * 256 + P:h * 256 + 2 * P], xh, inv(i, h, 1), start=True,
                                            stop=True, skip_group_check=True)
                        ins.then_inc(E("t_done"), 1)
                for i in range(3):
                    for h in range(2):
                        ins = pe.matmul(bank_x(i)[:, h * 64:h * 64 + 64], scores(i, h)[:, 256:384],
                                        vpad(i, h)[:, h * 64:h * 64 + 64], start=True, stop=True, skip_group_check=True)
                    ins.then_inc(E("mv_done"), 1)
                for i in range(3):
                    pe.wait_ge(E("inverse_ready"), c * 21 + 18 + i + 1)
                    pe.wait_ge(E("mv_kept"), 3 * c + i + 1)
                    for h in range(2):
                        ins = pe.matmul(bank_t(i)[:, h * P:h * P + P], inv(i, h, 1),
                                        seqmaj(i)[:, 0:4:3, h * 64:h * 64 + 64], start=True, stop=True,
                                        skip_group_check=True)
                    ins.then_inc(E("zu_done"), 1)
                for i in range(3):
                    pe.wait_ge(E("zu_kept"), 2 * (3 * c + i) + 2)
                    for h in range(2):
                        pe.matmul(bank_x(i)[:, 0:128], zupad(i, h, 0), scores(i, h)[:, 128:256], start=(h == 0),
                                  stop=(h == 1), skip_group_check=True)
                    for h in range(2):
                        ins = pe.matmul(bank_x(i)[:, 128:256], zupad(i, h, 0), seqmaj(i)[:, 1, :], start=(h == 0),
                                        stop=(h == 1), skip_group_check=True)
                    ins.then_inc(E("rg_done"), 1)
                for i in range(3):
                    o = bank_t(i)[:, 0:128]
                    for h in range(2):
                        pe.matmul(o, zupad(i, h, 1), scores(i, h)[:, 128:256], start=(h == 0), stop=False,
                                  skip_group_check=True)
                        pe.matmul(o, vpad(i, h), scores(i, h)[:, 384:512], start=False, stop=False,
                                  skip_group_check=True)
                    pe.wait_ge(E("state_scaled"), 3 * c + i + 1)
                    pe.wait_ge(E("r_ready"), 3 * c + i + 1)
                    pe.wait_ge(E("g_ready"), 3 * c + i + 1)
                    pe.matmul(o, s_scaled(i), rbuf(i), start=False, stop=True, skip_group_check=True)
                    n = bank_x(i)[:, 0:128]
                    pe.matmul(n, seqmaj(i)[:, 2, :], v_both(i), start=True, stop=False, skip_group_check=True)
                    pe.matmul(n, seqmaj(i)[:, 1, :], zu_both(i, 1), start=False, stop=False, skip_group_check=True)
                    pe.matmul(n, gbuf(i), s_scaled(i), start=False, stop=False, skip_group_check=True)
                    pe.matmul(n, const("ident"), s_scaled(i), start=False, stop=True,
                              skip_group_check=True).then_inc(E("chunk_done"), 1)
            pe.wait_ge(E("o_kept"), 3 * NC)
            pe.wait_ge(E("state_new"), 3 * NC)

        def after_core_sp(sp):
            sp.wait_ge(E("chunk_done"), 3 * NC)
            for m in range(8):
                sp.dma_start(w(32 + m), a["w_out"][m]).then_inc(E("wo_in"), 16)
            sp.wait_ge(E("state_new"), 3 * NC)
            ffn_sp(sp, 0, a["w_up"], a["w_down"])

        def after_core_pe(pe):
            for i in range(3):
                stats_matmuls(pe, f"gm{i}", Z + i, 1, const("block_mean"), None)
                stats_matmuls(pe, f"gv{i}", RR + i, 1, const("block_mean"), ("gn_squares", i))
            pe.wait_ge(E("wo_in"), 16 * 8)
            pe.wait_ge(E("y_c"), 3)
            for m in range(8):
                linear(pe, f"o{m}", lambda k, m=m: w(32 + m)[:, k * P:(k + 1) * P], Y1)
            stats_matmuls(pe, "ss2", [SQ2[0]], 1, const("ones"), ("square_sums", 6))
            ffn_pe(pe, 0)
            pe.wait_ge(E("ffn_out"), 8)
            stats_matmuls(pe, "ssf", [SQF[0]], 1, const("ones"), ("square_sums", 13))

        SQF = (11, 12, 13, 14, 15, 45, 46, 8)
        SQ2 = (26, 27, 28, 29, 30, 31, 18, 19)

        def rms_act(act, squares, wait_x, k_rstd):
            for k in range(8):
                act.wait_ge(E(wait_x[0]), wait_x[1] + k + 1)
                did(act, act.activation(w(squares[k]), w(X + k), ACT.Square), "squares")
            act.wait_ge(E("rstd_recip"), k_rstd)
            did(act, act.activation(w(RSTD), w(RSTD), ACT.Sqrt), "rstd_sqrt")

        def after_core_act(act):
            for i in range(3):
                act.wait_ge(E("pt_emptied_dve"), ordinal[f"gm{i}"])
                did(act, act.activation(w(RR + i), w(Z + i), ACT.Square), "gn_squares")
                act.wait_ge(E("gn_recip"), i + 1)
                did(act, act.activation(w(RR + i), w(RR + i), ACT.Sqrt), "gn_sqrt")
            rms_act(act, SQ2, ("pt_emptied_dve", ordinal["o0"] - 1), 2)
            for k in range(8):
                act.wait_ge(E("h_scaled"), 8 + k + 1)
                did(act, act.activation(hi(H + k), w(SQ2[k]), ACT.Identity, bias=small(MOD + 24 + k)), "h2_hi")
            ffn_act(act, 0, "ffn_conv_w", "ffn_conv_b")
            rms_act(act, SQF, ("ffn_out", 0), 3)

        def after_core_dve(dve):
            def V_(ins, name="dve_step"):
                return did(dve, ins, name)

            for i in range(3):
                dve.wait_ge(E("o_kept"), 3 * (NC - 1) + i + 1)
                filled(dve, f"gm{i}")
                V_(dve.tensor_tensor(w(Z + i), w(Z + i), pt(f"gm{i}")[:, :], ALU.subtract), "pt_emptied_dve")
                filled(dve, f"gv{i}")
                V_(dve.tensor_scalar(w(RR + i), pt(f"gv{i}")[:, :], GN_EPS, None, ALU.add), "pt_emptied_dve")
                V_(dve.reciprocal(w(RR + i), w(RR + i)), "gn_recip")
                dve.wait_ge(E("gn_sqrt"), i + 1)
                V_(dve.scalar_tensor_tensor(w(Z + i), w(Z + i), col("rwkv_ln_w", i), w(RR + i), ALU.mult, ALU.mult))
                V_(dve.scalar_tensor_tensor(w(Z + i), w(Z + i), col("rwkv_ln_b", i), w(BV + i), ALU.add, ALU.add))
                V_(dve.tensor_tensor(w(B + i), w(Z + i), w(GG[i]), ALU.mult), "y_c")
            for m in range(8):
                filled(dve, f"o{m}")
                V_(dve.scalar_tensor_tensor(w(X + m), pt(f"o{m}")[:, :], small(MOD + 16 + m), w(X + m), ALU.mult, ALU.add),
                   "pt_emptied_dve")
                add_square(dve, SQ2, 8, m - 1)
            add_square(dve, SQ2, 8, 7)
            filled(dve, "ss2")
            V_(dve.tensor_scalar(w(RSTD), pt("ss2")[:, :], 1.0 / D, EPS, ALU.mult, ALU.add), "pt_emptied_dve")
            V_(dve.reciprocal(w(RSTD), w(RSTD)), "rstd_recip")
            dve.wait_ge(E("rstd_sqrt"), 2)
            for k in range(9):
                if k < 8:
                    V_(dve.scalar_tensor_tensor(w(SQ2[k]), w(X + k), small(G2 + k), w(RSTD), ALU.mult, ALU.mult),
                       "h_scaled")
                if k > 0:
                    dve.wait_ge(E("h2_hi"), k)
                    V_(dve.scalar_tensor_tensor(lo(HLO, k - 1), w(SQ2[k - 1]), small(MOD + 24 + k - 1),
                                                hi(H + k - 1).bitcast(F32),
                                                ALU.add, ALU.subtract), "ffn_rhs_split")
            ffn_dve(dve, 0, "ffn_conv_w", lambda m: small(MOD + 40 + m), None)
            rms_dve(dve, "ssf", 3, lambda k: col("norm_final", k), X, "x2")

        def add_square(dve, squares, base, k):
            if k >= 1:
                dve.wait_ge(E("squares"), base + k + 1)
                did(dve, dve.tensor_tensor(w(squares[0]), w(squares[0]), w(squares[k]), ALU.add), "square_sums")

        XSUM = (37, 11)

        def add_x(dve, t, k):
            if k >= 1:
                acc = w(XSUM[t])
                did(dve, dve.tensor_tensor(acc, w(X) if k == 1 else acc, w(X + k), ALU.add), "x_sums")

        def rms_dve(dve, name, n, gain, dst, sem):
            filled(dve, name)
            did(dve, dve.tensor_scalar(w(RSTD), pt(name)[:, :], 1.0 / D, EPS, ALU.mult, ALU.add), "pt_emptied_dve")
            did(dve, dve.reciprocal(w(RSTD), w(RSTD)), "rstd_recip")
            dve.wait_ge(E("rstd_sqrt"), n)
            for k in range(8):
                did(dve, dve.scalar_tensor_tensor(w(dst + k), w(X + k), gain(k), w(RSTD), ALU.mult, ALU.mult), sem)

        UPRAW, UPHI, UPLO, HLO = 42, 44, 46, 38
        DNW = (42, 8)
        HID = 16

        def hi(slot):
            return HR[:, slot - H, :] if slot < H + 8 else WR[:, slot - UPHI, :]

        def top(slot):
            return hi(slot).bitcast(BF16)[:, 1:2 * S:2]

        def lo(slot, i):
            return w(slot + i // 2).bitcast(BF16)[:, (i % 2) * S:(i % 2) * S + S]

        def dn_weights(u):
            return W[:, DNW[u]:DNW[u] + 3, :].rearrange("p a n -> p (a n)")[:, 0:FT * P]

        def ffn_sp(sp, t, up, down):
            def load_down(m):
                sp.dma_start(dn_weights(m % 2), down[m]).then_inc(E(f"ffn_down_in{m % 2}"), 16)

            for g in range(2):
                sp.dma_start(w(UPRAW + g), up[0, :, g, :]).then_inc(E(f"ffn_up_in{g}"), 16)
            with sp.Fori(1, FT) as i:
                for g in range(2):
                    sp.wait_ge(E("ffn_up_split"), i * 2 + (g - 1 + 2 * FT * t))
                    sp.dma_start(w(UPRAW + g), up[bass.ds(i, 1)].rearrange("a p g n -> (a p) g n")[:, g, :])\
                        .then_inc(E(f"ffn_up_in{g}"), 16)
            sp.wait_ge(E("ffn_up_split"), 2 * FT * (t + 1))
            sp.wait_ge(E("ffn_gate_filled"), FT * (t + 1))
            load_down(0)
            sp.wait_ge(E("ffn_val_filled"), FT * (t + 1))
            load_down(1)
            for m in range(2, 8):
                sp.wait_ge(E("ffn_down_filled"), m - 1 + 8 * t)
                load_down(m)

        def ffn_pool(pool, t):
            def up(j, first):
                for g in range(2):
                    if not first:
                        pool.wait_ge(E("ffn_gate_filled" if g == 0 else "ffn_val_filled"), j + FT * t)
                    pool.wait_ge(E(f"ffn_up_in{g}"), j * 16 + (16 + 16 * FT * t))
                    pool.tensor_tensor(hi(UPHI + g).rearrange("p (k n) -> p k n", n=P),
                                       w(UPRAW + g).rearrange("p (k n) -> p k n", n=P),
                                       const("ones").unsqueeze(1).to_broadcast([P, DT, P]), ALU.mult)\
                        .then_inc(E("ffn_up_hi"), 1)
                    pool.wait_ge(E("ffn_up_hi"), j * 2 + (g + 1 + 2 * FT * t))
                    pool.tensor_tensor(lo(UPLO, g), w(UPRAW + g), hi(UPHI + g).bitcast(F32), ALU.subtract)\
                        .then_inc(E("ffn_up_split"), 1)

            up(0, True)
            with pool.Fori(1, FT) as j:
                up(j, False)

        def ffn_pe(pe, t):
            for e in ("dve", "act"):
                pe.wait_ge(E(f"pt_emptied_{e}"), counts_before[t][e])

            def up(j, first):
                for u in range(2):
                    for g in range(2):
                        pe.wait_ge(E("ffn_up_split"), j * 4 + (2 * u + g + 1 + 2 * FT * t))
                        if g == 0 and not first:
                            pe.wait_ge(E("ffn_hidden"), j * 2 + (u - 1 + FT * t))
                        for h in range(2):
                            out = PT[2 * u + g][:, h * 512:h * 512 + 512]
                            seq = slice(h * 512, h * 512 + 512)
                            for k in range(8):
                                if first and u == 0 and g == 0 and h == 0:
                                    pe.wait_ge(E("ffn_rhs_split"), 8 * t + k + 1)
                                cols = slice(k * P, (k + 1) * P)
                                pe.matmul(out, hi(UPHI + g)[:, cols], hi(H + k)[:, seq], start=(k == 0), stop=False)
                                pe.matmul(out, top(UPHI + g)[:, cols], lo(HLO, k)[:, seq], start=False, stop=False)
                                ins = pe.matmul(out, lo(UPLO, g)[:, cols], top(H + k)[:, seq], start=False,
                                                stop=(k == 7))
                        ins.then_inc(E("ffn_gate_filled" if g == 0 else "ffn_val_filled"), 1)

            up(0, True)
            with pe.Fori(1, FT // 2) as j:
                up(j, False)

            def down(j, first):
                for u in range(2):
                    pe.wait_ge(E(f"ffn_down_in{u}"), j * 16 + (16 + 64 * t))
                    if not first:
                        pe.wait_ge(E("ffn_out"), j * 2 + (u - 1 + 8 * t))
                    for h in range(2):
                        for f in range(FT):
                            if first and u == 0 and h == 0 and f in (0, FT - 1):
                                pe.wait_ge(E("ffn_hidden"), (FT - 1 if f == 0 else FT) + FT * t)
                            ins = pe.matmul(PT[u][:, h * 512:h * 512 + 512], dn_weights(u)[:, f * P:(f + 1) * P],
                                            w(HID + f)[:, h * 512:h * 512 + 512], start=(f == 0), stop=(f == FT - 1))
                    ins.then_inc(E("ffn_down_filled"), 1)

            down(0, True)
            with pe.Fori(1, 4) as j:
                down(j, False)

        def ffn_act(act, t, cw, cb):
            def body(j):
                for u in range(2):
                    i = j * 2 + u
                    hid = W[:, bass.ds(i + HID, 1), :].rearrange("p a n -> p (a n)")
                    act.wait_ge(E("par_in"), 32)
                    act.wait_ge(E("ffn_gate_filled"), i + (1 + FT * t))
                    act.activation(hid, PT[2 * u][:, :], ACT.Identity, bias=par[:, bass.ds(i + COL[cb], 1)],
                                   scale=par[:, bass.ds(i + (COL[cw] + 2 * FT), 1)]).then_inc(E("ffn_tap"), 1)
                    act.wait_ge(E("par_in"), 32)
                    act.wait_ge(E("ffn_conv"), i + (1 + FT * t))
                    act.activation(hid, hid, ACT.Silu).then_inc(E("ffn_silu"), 1)

            with act.Fori(0, FT // 2) as j:
                body(j)

        def ffn_dve(dve, t, cw, gain, alpha):
            def body(j):
                for u in range(2):
                    i = j * 2 + u
                    hid = W[:, bass.ds(i + HID, 1), :].rearrange("p a n -> p (a n)")
                    g = PT[2 * u]
                    dve.wait_ge(E("ffn_tap"), i + (1 + FT * t))
                    dve.scalar_tensor_tensor(hid[:, 1:], g[:, :S - 1], par[:, bass.ds(i + (COL[cw] + FT), 1)], hid[:, 1:],
                                             ALU.mult, ALU.add).then_inc(E("ffn_conv1"), 1)
                    dve.wait_ge(E("ffn_conv1"), i + (1 + FT * t))
                    dve.scalar_tensor_tensor(hid[:, 2:], g[:, :S - 2], par[:, bass.ds(i + COL[cw], 1)], hid[:, 2:],
                                             ALU.mult, ALU.add).then_inc(E("ffn_conv"), 1)
                    dve.wait_ge(E("ffn_silu"), i + (1 + FT * t))
                    dve.wait_ge(E("ffn_val_filled"), i + (1 + FT * t))
                    dve.tensor_tensor(hid, hid, PT[2 * u + 1][:, :], ALU.mult).then_inc(E("ffn_hidden"), 1)

            with dve.Fori(0, FT // 2) as j:
                body(j)

            for m in range(8):
                dve.wait_ge(E("ffn_down_filled"), m + 1 + 8 * t)
                if t == 0:
                    ins = dve.scalar_tensor_tensor(w(X + m), PT[m % 2][:, :], gain(m), w(X + m), ALU.mult, ALU.add)
                else:
                    ins = dve.scalar_tensor_tensor(w(X + m), w(X + m), alpha, PT[m % 2][:, :], ALU.mult, ALU.add)
                did(dve, ins, "ffn_out")
                if t == 0:
                    add_square(dve, SQF, 16, m - 1)
                else:
                    add_x(dve, 1, m)
            if t == 0:
                add_square(dve, SQF, 16, 7)

        UST, COS_, SIN_, BR, BRS = 8, 12, 13, 14, 15
        Q2, K2, CLS, TMP, V2, GATE, VW = 16, 18, 24, 25, 26, 30, 34
        XT_, XST, TP, P1, P2, GS = 42, 43, 44, 45, 46, 47
        RING2 = 38
        flat20 = W[:, 20:23, :].rearrange("p a n -> p (a n)")
        CL = flat20[:, 0:1152].rearrange("p (g j c) -> p g j c", g=8, j=9)
        BPAD = flat20[:, 1152:2288]
        PWR = flat20[:, 2288:2576].rearrange("p (j g) -> p j g", j=9)
        PWI = flat20[:, 2576:2864].rearrange("p (j g) -> p j g", j=9)
        QR = w(23)[:, 0:256].rearrange("p (j g) -> p j g", j=8)
        QI = w(23)[:, 256:512].rearrange("p (j g) -> p j g", j=8)
        B1 = w(40)[:, 0:512].rearrange("p (g c) -> p g c", g=32)
        B2 = w(40)[:, 512:1024].rearrange("p (g c) -> p g c", g=32)
        C1 = w(41)[:, 0:512].rearrange("p (g c) -> p g c", g=32)
        C2 = w(41)[:, 512:1024].rearrange("p (g c) -> p g c", g=32)

        def s5c(n):
            return w(23)[:, 512 + 32 * n:544 + 32 * n]

        LRE, LIM, DTC, DCOL, XRE, TURN, TA, TB_, TC_, CR, CI, T8 = range(12)
        NROW = flat20[:, 2864:2992]
        GLUW = 40
        RETC, KP, QX, KZ = 23, 12, (20, 21), (34, 35, 44, 45)
        STB, SCS = (22, 36), (37, 42, 43, 46)
        TS = (42, 43, 46, 47)
        WO2 = (16, 17, 18, 19, 20, 21, 24, 25)
        Y2 = (8, 9, 10, 11, 30, 31, 32, 33)
        ring2 = [it for it in ORDER2 if isinstance(it, str) and it in PROJ2]

        def mixer2_sp(sp):
            sp.wait_ge(E("ffn_out"), 8)
            for n, it in enumerate(ring2):
                if n >= 2:
                    sp.wait_ge(E("pt_filled"), place["b2" + ring2[n - 2]] + 1)
                sp.dma_start(w(RING2 + n % 2), a["w_in_2"][PROJ2[it]]).then_inc(E(f"ring2_{n % 2}"), 16)
                if n == 1:
                    sp.dma_start(w(23)[:, 512:640], a["s5_cols"]).then_inc(E("s5_in"), 16)
                    sp.dma_start(W[:, 40:42, :], a["s5_bc"]).then_inc(E("s5_in"), 16)
                    sp.dma_start(NROW, a["n_row"]).then_inc(E("s5_in"), 16)
                    sp.dma_start(W[:, VW:VW + 4, :], a["w_v_2"]).then_inc(E("v2_in"), 16)
                if it == "q0":
                    for q in range(4):
                        sp.wait_ge(E("pt_emptied_act"), ordinal[f"b2u{q}"])
                        sp.dma_start(a["u_scratch"][q * P:(q + 1) * P], w(UST + q)).then_inc(E("u_out"), 16)
                    sp.wait_ge(E("u_out"), 64)
                    us = a["u_scratch"].rearrange("(g c) (s n) -> s c g n", c=16, s=8)
                    for s in range(8):
                        sp.dma_start(W[16 * s:16 * s + 16, UST:UST + 4, :].rearrange("p a (g n) -> p (a g) n", n=P),
                                     us[s]).then_inc(E("u_back"), 16)
            for q in range(4):
                sp.wait_ge(E("y_out"), 128 * (q + 1))
                sp.dma_start(w(UST + q), a["y_scratch"][q * P:(q + 1) * P]).then_inc(E("y_back"), 16)
            sp.wait_ge(E("pt_filled"), place["yy3"] + 1)
            sp.dma_start(W[:, GLUW:GLUW + 2, :], a["w_glu"]).then_inc(E("glu_in"), 16)
            sp.dma_start(W[:, CLS:CLS + 2, :], a["rope"]).then_inc(E("rope_in"), 16)
            sp.dma_start(w(RETC)[:, 0:768], a["ret"]).then_inc(E("ret_in"), 16)
            sp.wait_ge(E("pt_filled"), place["ro3"] + 1)
            sp.wait_ge(E("rotated"), 4)
            for m in range(8):
                sp.dma_start(w(WO2[m]), a["w_out_2"][m]).then_inc(E("wo2_in"), 16)
            sp.wait_ge(E("y_ret"), 4)
            ffn_sp(sp, 1, a["w_up_2"], a["w_down_2"])
            for k in range(8):
                sp.wait_ge(E("x4_ready"), k + 1)
                sp.dma_start(a["out"][:, k, :], w(X + k)).then_inc(E("out"), 16)
            sp.wait_ge(E("out"), 128)

        def mixer2_pool(pool):
            def G_(ins, name="pool_step"):
                return did(pool, ins, name)

            pool.wait_ge(E("ffn_out"), 8)
            pool.wait_ge(E("x2"), 8)
            G_(pool.memset(BPAD, 0.0))
            G_(pool.memset(w(P1), 0.0), "s5_zeroed")
            G_(pool.memset(w(P2), 0.0), "s5_zeroed")
            pool.wait_ge(E("s5_coefs"), 1)
            for q in range(4):
                gs = slice(8 * q, 8 * q + 8)
                sh = [P, 8, 8, 16]

                def bc(m):
                    return m[:, gs, :].unsqueeze(2).to_broadcast(sh)

                def pw(m, rev, j0=0):
                    v = m[:, j0:j0 + 8, gs]
                    if rev:
                        v = m[:, 7::-1, gs]
                    return v.rearrange("p j g -> p g j").unsqueeze(3).to_broadcast(sh)

                def view(slot):
                    return w(slot).rearrange("p (g j c) -> p g j c", g=8, j=8)

                if q > 0:
                    pool.wait_ge(E("pt_filled"), place[f"brs{q - 1}"] + 1)
                    pool.wait_ge(E("s5_demod"), q)
                for dst, m1, m2, op, sem in ((BR, QR, QI, ALU.add, "br_ready"), (BRS, QI, QR, ALU.subtract, "brs_ready")):
                    G_(pool.tensor_tensor(view(dst), bc(B1), pw(m1, True), ALU.mult))
                    G_(pool.tensor_tensor(view(TMP), bc(B2), pw(m2, True), ALU.mult))
                    G_(pool.tensor_tensor(view(dst), view(dst), view(TMP), op), sem)
                if q > 0:
                    pool.wait_ge(E("pt_filled"), place[f"tp{q - 1}"] + 1)
                bp = BPAD[:, 112:1136].rearrange("p (g n) -> p g n", n=P)[:, :, 0:16]
                G_(pool.tensor_copy(bp, view(BR)[:, :, 7, :]), "pool_step")
                if q > 0:
                    pool.wait_ge(E("pt_filled"), place[f"yy{q - 1}"] + 1)
                for j0, dst, m1, m2, op, sem in ((1, CL[:, :, 1:9, :], PWR, PWI, ALU.add, "cl_ready"),
                                                 (1, view(CLS), PWI, PWR, ALU.subtract, "pool_step")):
                    x, y = (C1, C2) if op == ALU.add else (C2, C1)
                    G_(pool.tensor_tensor(dst, bc(x), pw(PWR, False, j0), ALU.mult))
                    G_(pool.tensor_tensor(view(TMP), bc(y), pw(PWI, False, j0), ALU.mult))
                    G_(pool.tensor_tensor(dst, dst, view(TMP), op), "pool_step")
                G_(pool.tensor_copy(CL[:, :, 0, :], C1[:, gs, :]), "cl_ready")

        def mixer2_pe(pe):
            xs = range(X, X + 8)
            ringn = [0]

            def proj2(it):
                n = ringn[0]
                ringn[0] += 1
                linear(pe, "b2" + it, lambda k: w(RING2 + n % 2)[:, k * P:(k + 1) * P], xs,
                       lambda: pe.wait_ge(E(f"ring2_{n % 2}"), 16 * (n // 2 + 1)),
                       ("x2", 0) if n == 0 else None)

            def per_group(name, fn):
                claim(pe, name)
                for g in range(8):
                    ins = fn(pt(name)[:, g * P:(g + 1) * P], g)
                ins.then_inc(E("pt_filled"), 1)

            def s5_step(step, q):
                def mm(o, l, r, start=True, stop=True):
                    return pe.matmul(o, l, r, start=start, stop=stop, skip_group_check=True)

                def grp(slot, g):
                    return w(slot)[:, g * P:(g + 1) * P]

                if step == "A":
                    pe.wait_ge(E("br_ready"), q + 1)
                    per_group(f"br{q}", lambda o, g: pe.transpose(o, grp(BR, g), const("ident")))
                    pe.wait_ge(E("brs_ready"), q + 1)
                    per_group(f"brs{q}", lambda o, g: pe.transpose(o, grp(BRS, g), const("ident")))
                    pe.wait_ge(E("cl_ready"), q + 1)

                    def toeplitz(o, g):
                        for s in range(8):
                            at = g * P + (7 - s) * 16
                            ins = mm(o[:, 16 * s:P], BPAD[:, at:at + P],
                                     CL[:, g, 0:8 - s, :].rearrange("p j c -> p (j c)"), s == 0, s == 7)
                        return ins

                    per_group(f"tp{q}", toeplitz)
                if step == "B":
                    pe.wait_ge(E("u_back"), 128)
                    pe.wait_ge(E("pt_emptied_act"), ordinal[f"brs{q}"])
                    per_group(f"xx{q}", lambda o, g: mm(o, grp(XT_, g), grp(UST + q, g)))
                    per_group(f"xs{q}", lambda o, g: mm(o, grp(XST, g), grp(UST + q, g)))
                if step == "C":
                    pe.wait_ge(E("tp_kept"), q + 1)
                    pe.wait_ge(E("s5_states"), q + 1)

                    def out(o, g):
                        mm(o, grp(TP, g), grp(UST + q, g), True, False)
                        mm(o, CL[:, g, 1:9, :].rearrange("p j c -> p (j c)"), grp(P1, g), False, False)
                        return mm(o, grp(CLS, g), grp(P2, g), False, True)

                    per_group(f"yy{q}", out)

            wv = W[:, VW:VW + 4, :].rearrange("p a (b n) -> p (a b) n", n=512)
            for it in ORDER2:
                if not isinstance(it, str):
                    s5_step(*it)
                elif it in PROJ2:
                    proj2(it)
                else:
                    v = int(it[1])
                    claim(pe, "b2" + it)
                    pe.wait_ge(E("v2_in"), 16)
                    for t in range(2):
                        for k in range(8):
                            st = 2 * v + t
                            ins = pe.matmul(pt("b2" + it)[:, t * 512:t * 512 + 512], w(X + k)[:, st * P:(st + 1) * P],
                                            wv[:, k, :], start=(k == 0), stop=(k == 7))
                    ins.then_inc(E("pt_filled"), 1)
            for i in range(4):
                linear(pe, f"swap{i}", lambda k: const("swap_halves"), [Q2 + i])
            pe.wait_ge(E("y_back"), 64)
            pe.wait_ge(E("glu_in"), 16)
            wg = W[:, GLUW:GLUW + 2, :].rearrange("p a (b n) -> p (a b) n", n=512)
            for m in range(4):
                linear(pe, f"glu{m}", lambda k, m=m: wg[:, m, k * P:(k + 1) * P], range(UST, UST + 4))
            stats_matmuls(pe, "ss5", KP, 4, const("ones"), ("s5_squares", 0))
            pe.wait_ge(E("rotated"), 4)
            for i in range(2):
                per_group(f"kt{i}", lambda o, st, i=i: pe.transpose(o, w(K2 + i)[:, st * P:(st + 1) * P], const("ident")))
            for i in range(2):
                for hh in range(2):
                    h = 2 * i + hh
                    pe.wait_ge(E("k_padded"), h + 1)
                    per_group(f"sc{h}", lambda o, st, h=h, i=i: pe.matmul(
                        o, w(KP + h)[:, st * P:(st + 1) * P], w(Q2 + i)[:, st * P:(st + 1) * P], start=True, stop=True,
                        skip_group_check=True))
                claim(pe, f"kv{i}")
                pe.wait_ge(E("pt_emptied_act"), ordinal[f"kt{i}"])
                pe.wait_ge(E("state2_zero"), 2)
                vseq = W[:, V2:V2 + 4, :].rearrange("p a (b n) -> p (a b) n", n=512)

                def kv(st):
                    if st >= 2:
                        pe.wait_ge(E("state2"), 32 * i + 4 * (st - 1))
                    for j in range(2):
                        ins = pe.matmul(pt(f"kv{i}")[:, (st % 2) * 512 + j * 256:(st % 2) * 512 + j * 256 + 256],
                                        w(KZ[2 * i + j])[:, st * P:(st + 1) * P], vseq[:, st, i * 256:i * 256 + 256],
                                        start=True, stop=True, skip_group_check=True)
                    ins.then_inc(E("kv_done"), 1)

                kv(0)
                for hh in range(2):
                    claim(pe, f"ro{2 * i + hh}")
                pe.wait_ge(E("pt_emptied_dve"), ordinal[f"sc{2 * i + 1}"])
                pe.wait_ge(E("qx_ready"), i + 1)
                for st in range(8):
                    if st < 7:
                        kv(st + 1)
                    pe.wait_ge(E("state2"), 32 * i + 4 * st + 2)
                    for hh in range(2):
                        h = 2 * i + hh
                        o = pt(f"ro{h}")[:, st * P:(st + 1) * P]
                        pe.matmul(o, vseq[:, st, h * P:(h + 1) * P], w(SCS[h])[:, st * P:(st + 1) * P], start=True,
                                  stop=False, skip_group_check=True)
                        for j in range(2):
                            n = 2 * st + j
                            ins = pe.matmul(o[:, j * 64:j * 64 + 64],
                                            w(STB[i])[:, (n % 4) * 256 + hh * P:(n % 4) * 256 + hh * P + P],
                                            w(QX[i])[:, n * 64:n * 64 + 64], start=False, stop=(j == 1),
                                            skip_group_check=True)
                        if st < 7:
                            if hh == 1:
                                ins.then_inc(E("ro_step"), 1)
                        else:
                            if hh == 0:
                                ins.then_inc(E("pt_filled"), 2)
                            else:
                                ins.then_inc(E("pt_filled"), 1)
            for h in range(4):
                pe.wait_ge(E("pt_emptied_act"), ordinal[f"ro{h}"])
                stats_matmuls(pe, f"rm{h}", SCS[h], 1, const("ones"), None)
                stats_matmuls(pe, f"rv{h}", KP + h, 1, const("ones"), ("ret_squares", h))
            pe.wait_ge(E("wo2_in"), 128)
            pe.wait_ge(E("y_ret"), 4)
            pe.wait_ge(E("y_s5"), 4)
            for m in range(8):
                linear(pe, f"p{m}", lambda k, m=m: w(WO2[m])[:, k * P:(k + 1) * P], Y2)
            for t, sq, base in ((1, range(26, 34), 24), (2, range(H, H + 8), 32)):
                if t == 2:
                    pe.wait_ge(E("ffn_out"), 16)
                stats_matmuls(pe, f"lm{t}", [XSUM[t - 1]], 1, const("ones"), ("x_sums", 7 * t - 1))
                stats_matmuls(pe, f"lv{t}", sq, 8, const("ones"), ("squares", base))
                if t == 1:
                    ffn_pe(pe, 1)

        def mixer2_act(act):
            def A_(dst, src, func, name, **kw):
                return did(act, act.activation(dst, src, func, **kw), name)

            TWO_PI = 6.283185
            ys = a["y_scratch"].rearrange("(g c) (s n) -> s c g n", c=16, s=8)
            act.wait_ge(E("s5_in"), 48)
            A_(s5c(DTC), s5c(DTC), ACT.Exp, "s5_dt")
            act.wait_ge(E("s5_power_args"), 1)
            A_(PWR, PWR, ACT.Sin, "act_step", scale=TWO_PI)
            A_(PWI, PWI, ACT.Sin, "act_step", scale=TWO_PI)
            A_(w(TMP)[:, 0:288], w(TMP)[:, 0:288], ACT.Exp, "s5_power_mag")

            def tables(q):
                act.wait_ge(E("s5_table_args"), q + 1)
                A_(w(SIN_), w(SIN_), ACT.Sin, "s5_tables", scale=TWO_PI)
                A_(w(COS_), w(COS_), ACT.Sin, "s5_tables", scale=TWO_PI)

            for it in ORDER2:
                if not isinstance(it, str):
                    step, q = it
                    if step == "A":
                        tables(q)
                        if q > 0:
                            act.wait_ge(E("pt_emptied_dve"), ordinal[f"xs{q - 1}"])
                        for nm, dst in (("br", XT_), ("brs", XST)):
                            filled(act, f"{nm}{q}")
                            A_(w(dst), pt(f"{nm}{q}")[:, :], ACT.Copy, "pt_emptied_act")
                    if step == "C":
                        filled(act, f"yy{q}")
                        if q < 3:
                            act.wait_ge(E("s5_table_args"), q + 2)
                        A_(w(GS), pt(f"yy{q}")[:, :], ACT.Gelu_apprx_tanh, "pt_emptied_act")
                        for s in range(8):
                            act.dma_start(ys[s][:, 8 * q:8 * q + 8],
                                          w(GS)[16 * s:16 * s + 16].rearrange("p (g n) -> p g n", n=P))\
                                .then_inc(E("y_out"), 16)
                    continue
                nm = "b2" + it
                filled(act, nm)
                if it[0] == "u":
                    A_(w(UST + int(it[1])).rearrange("p (s n) -> p s n", s=8),
                       pt(nm)[:, :].rearrange("p (n s) -> p s n", s=8), ACT.Copy, "pt_emptied_act")
                elif it[0] in "qk":
                    A_(w((Q2 if it[0] == "q" else K2) + int(it[1])), pt(nm)[:, :], ACT.Copy, "pt_emptied_act")
                elif it[0] == "v":
                    A_(w(V2 + int(it[1])), pt(nm)[:, :], ACT.Copy, "pt_emptied_act")
                else:
                    A_(w(GATE + int(it[1])), pt(nm)[:, :], ACT.Silu, "pt_emptied_act")
            act.wait_ge(E("y_out"), 512)
            for m in range(4):
                filled(act, f"glu{m}")
                A_(w(TS[m]), pt(f"glu{m}")[:, :], ACT.Sigmoid, "pt_emptied_act", bias=col("s5_glu_b_2", m))
            for m in range(4):
                act.wait_ge(E("s5_gated"), m + 1)
                A_(w(KP + m), w(TS[m]), ACT.Square, "s5_squares")
            act.wait_ge(E("s5_recip"), 1)
            A_(w(22), w(22), ACT.Sqrt, "s5_rstd")
            for i in range(2):
                filled(act, f"kt{i}")
                src = pt(f"kt{i}")[:, :].rearrange("p (s h n) -> p s h n", s=8, h=2)
                for j in range(2):
                    for hh in range(2):
                        dst = w(KZ[2 * i + j]).rearrange("p (s h n) -> p s h n", s=8, h=2)[:, :, hh, :]
                        last = i * 2 + hh
                        A_(dst, src[:, :, hh, :], ACT.Copy, "pt_emptied_act" if j * hh else "act_step",
                           scale=const("ret_zeta")[:, 4 * j + last:4 * j + last + 1])
            for h in range(4):
                filled(act, f"ro{h}")
                A_(w(SCS[h]), pt(f"ro{h}")[:, :], ACT.Copy, "pt_emptied_act")
            for h in range(4):
                act.wait_ge(E("pt_emptied_dve"), ordinal[f"rm{h}"])
                A_(w(KP + h), w(SCS[h]), ACT.Square, "ret_squares")
                act.wait_ge(E("ret_recip"), h + 1)
                A_(w(KP + h), w(KP + h), ACT.Sqrt, "ret_sqrt")
            for t, sq in ((1, range(26, 34)), (2, range(H, H + 8))):
                for k in range(8):
                    act.wait_ge(E("centered"), 8 * (t - 1) + k + 1)
                    A_(w(sq[k]), w(X + k), ACT.Square, "squares")
                act.wait_ge(E("rstd_recip"), 3 + t)
                A_(w(RSTD), w(RSTD), ACT.Sqrt, "rstd_sqrt")
                for k in range(8):
                    act.wait_ge(E("ln_scaled"), 8 * (t - 1) + k + 1)
                    A_(w(X + k), w(X + k), ACT.Identity, f"x{2 + t}_ready", bias=col(f"ln{t}_b_2", k))
                    if t == 1:
                        A_(hi(H + k), w(X + k), ACT.Copy, "x3_hi")
                if t == 1:
                    ffn_act(act, 1, "ffn_conv_w_2", "ffn_conv_b_2")

        def mixer2_dve(dve):
            def V_(ins, name="dve_step"):
                return did(dve, ins, name)

            c = s5c
            dve.wait_ge(E("s5_dt"), 1)
            V_(dve.tensor_tensor(c(XRE), c(LRE), c(DTC), ALU.mult))
            V_(dve.tensor_tensor(c(TURN), c(LIM), c(DTC), ALU.mult))
            V_(dve.tensor_scalar(c(TA), c(TURN), 1.0 / (2 * np.pi), RND, ALU.mult, ALU.add))
            V_(dve.tensor_scalar(c(TA), c(TA), RND, None, ALU.subtract))
            V_(dve.scalar_tensor_tensor(c(TURN), c(TA), -6.28125, c(TURN), ALU.mult, ALU.add))
            V_(dve.scalar_tensor_tensor(c(TURN), c(TA), -(2 * np.pi - 6.28125), c(TURN), ALU.mult, ALU.add))
            V_(dve.tensor_scalar(c(TURN), c(TURN), 1.0 / (2 * np.pi), None, ALU.mult))

            def frac(dst, tmp):
                V_(dve.tensor_scalar(tmp, dst, RND, RND, ALU.add, ALU.subtract))
                V_(dve.tensor_tensor(dst, dst, tmp, ALU.subtract))

            sh = [P, 9, 32]
            jrow = NROW[:, 0:9].unsqueeze(2).to_broadcast(sh)
            tmp = w(TMP)[:, 0:288].rearrange("p (j g) -> p j g", j=9)
            tmp2 = w(TMP)[:, 288:576].rearrange("p (j g) -> p j g", j=9)
            V_(dve.tensor_tensor(PWI, jrow, c(TURN).unsqueeze(1).to_broadcast(sh), ALU.mult))
            frac(PWI, tmp)
            V_(dve.tensor_scalar(PWR, PWI, 0.25, None, ALU.add))
            frac(PWR, tmp)
            V_(dve.tensor_tensor(tmp, jrow, c(XRE).unsqueeze(1).to_broadcast(sh), ALU.mult), "s5_power_args")
            V_(dve.tensor_scalar(c(T8), c(TURN), 8.0, None, ALU.mult))
            frac(c(T8), c(TA))
            dve.wait_ge(E("s5_power_mag"), 1)
            V_(dve.tensor_tensor(PWR, PWR, tmp, ALU.mult))
            V_(dve.tensor_tensor(PWI, PWI, tmp, ALU.mult))
            V_(dve.tensor_copy(c(XRE), tmp[:, 8, :]))
            V_(dve.tensor_tensor(c(TA), c(LRE), c(LRE), ALU.mult))
            V_(dve.tensor_tensor(c(TB_), c(LIM), c(LIM), ALU.mult))
            V_(dve.tensor_tensor(c(TA), c(TA), c(TB_), ALU.add))
            V_(dve.reciprocal(c(TA), c(TA)))
            V_(dve.tensor_scalar(c(TB_), PWR[:, 1, :], -1.0, None, ALU.add))
            V_(dve.tensor_tensor(c(CR), c(TB_), c(LRE), ALU.mult))
            V_(dve.tensor_tensor(c(TC_), PWI[:, 1, :], c(LIM), ALU.mult))
            V_(dve.tensor_tensor(c(CR), c(CR), c(TC_), ALU.add))
            V_(dve.tensor_tensor(c(CR), c(CR), c(TA), ALU.mult))
            V_(dve.tensor_tensor(c(CI), PWI[:, 1, :], c(LRE), ALU.mult))
            V_(dve.tensor_tensor(c(TC_), c(TB_), c(LIM), ALU.mult))
            V_(dve.tensor_tensor(c(CI), c(CI), c(TC_), ALU.subtract))
            V_(dve.tensor_tensor(c(CI), c(CI), c(TA), ALU.mult))
            sh8 = [P, 8, 32]
            crb, cib = (c(x).unsqueeze(1).to_broadcast(sh8) for x in (CR, CI))
            t8 = tmp[:, 0:8, :]
            V_(dve.tensor_tensor(QR, PWR[:, 0:8, :], crb, ALU.mult))
            V_(dve.tensor_tensor(t8, PWI[:, 0:8, :], cib, ALU.mult))
            V_(dve.tensor_tensor(QR, QR, t8, ALU.subtract))
            V_(dve.tensor_tensor(QI, PWR[:, 0:8, :], cib, ALU.mult))
            V_(dve.tensor_tensor(t8, PWI[:, 0:8, :], crb, ALU.mult))
            V_(dve.tensor_tensor(QI, QI, t8, ALU.add))
            V_(dve.tensor_scalar(w(40)[:, 512:1024], w(40)[:, 512:1024], const("sgn_re"), None, ALU.mult))
            V_(dve.tensor_scalar(w(41)[:, 0:512], w(41)[:, 0:512], const("sgn_im"), None, ALU.mult))
            V_(dve.tensor_scalar(w(41)[:, 512:1024], w(41)[:, 512:1024], -1.0, None, ALU.mult), "s5_coefs")

            def g3(ap):
                return ap.rearrange("p (g n) -> p g n", g=8)

            def tables(q):
                if q > 0:
                    dve.wait_ge(E("s5_states"), q)
                gs = slice(8 * q, 8 * q + 8)
                s8 = [P, 8, P]
                t = w(COS_)
                V_(dve.tensor_tensor(g3(w(SIN_)), NROW.unsqueeze(1).to_broadcast(s8),
                                     c(T8)[:, gs].unsqueeze(2).to_broadcast(s8), ALU.mult))
                V_(dve.tensor_scalar(t, w(SIN_), RND, RND, ALU.add, ALU.subtract))
                V_(dve.tensor_tensor(w(SIN_), w(SIN_), t, ALU.subtract))
                V_(dve.tensor_scalar(t, w(SIN_), 0.25, None, ALU.add))
                V_(dve.tensor_scalar(w(GS), t, RND, RND, ALU.add, ALU.subtract))
                V_(dve.tensor_tensor(t, t, w(GS), ALU.subtract), "s5_table_args")

            tables(0)
            for it in ORDER2:
                if isinstance(it, str):
                    continue
                step, q = it
                gs = slice(8 * q, 8 * q + 8)
                if step == "A":
                    filled(dve, f"tp{q}")
                    if q > 0:
                        dve.wait_ge(E("pt_filled"), place[f"yy{q - 1}"] + 1)
                    V_(dve.tensor_tensor(g3(w(TP)), const("ident").unsqueeze(1).to_broadcast([P, 8, P]),
                                         c(DCOL)[:, gs].unsqueeze(2).to_broadcast([P, 8, P]), ALU.mult))
                    V_(dve.tensor_tensor(w(TP), w(TP), pt(f"tp{q}")[:, :], ALU.add), "pt_emptied_dve")
                    V_(dve.tensor_copy(c(TB_), c(TA)), "tp_kept")
                if step == "B":
                    dve.wait_ge(E("s5_tables"), 2 * (q + 1))
                    if q > 0:
                        dve.wait_ge(E("y_out"), 128 * q)
                    filled(dve, f"xx{q}")
                    V_(dve.tensor_tensor(w(GS), pt(f"xx{q}")[:, :], w(COS_), ALU.mult), "pt_emptied_dve")
                    filled(dve, f"xs{q}")
                    V_(dve.tensor_tensor(w(BRS), pt(f"xs{q}")[:, :], w(SIN_), ALU.mult), "pt_emptied_dve")
                    V_(dve.tensor_tensor(w(GS), w(GS), w(BRS), ALU.add), "s5_demod")
                    for g in range(8):
                        gg = w(GS)[:, g * P:(g + 1) * P]
                        V_(dve.tensor_tensor_scan(gg, c(XRE)[:, 8 * q + g:8 * q + g + 1].to_broadcast([P, P]), gg, 0.0,
                                                  ALU.mult, ALU.add))
                    if q == 0:
                        dve.wait_ge(E("s5_zeroed"), 2)
                    else:
                        dve.wait_ge(E("pt_filled"), place[f"yy{q - 1}"] + 1)
                    V_(dve.tensor_tensor(g3(w(P1))[:, :, 1:], g3(w(GS))[:, :, :P - 1], g3(w(COS_))[:, :, :P - 1], ALU.mult))
                    V_(dve.tensor_tensor(g3(w(P2))[:, :, 1:], g3(w(GS))[:, :, :P - 1], g3(w(SIN_))[:, :, :P - 1], ALU.mult),
                       "s5_states")
                    if q < 3:
                        tables(q + 1)
            dve.wait_ge(E("rope_in"), 16)
            for i in range(4):
                s = w(Q2 + i)
                filled(dve, f"swap{i}")
                V_(dve.tensor_tensor(w(44), pt(f"swap{i}")[:, :], w(CLS + 1), ALU.mult), "pt_emptied_dve")
                V_(dve.tensor_tensor(s, s, w(CLS), ALU.mult))
                V_(dve.tensor_tensor(s, s, w(44), ALU.add), "rotated")
            dve.wait_ge(E("pt_emptied_act"), ordinal["glu3"])
            for m in range(4):
                V_(dve.tensor_tensor(w(TS[m]), w(TS[m]), w(UST + m), ALU.mult), "s5_gated")
            dve.wait_ge(E("ret_in"), 16)
            filled(dve, "ss5")
            V_(dve.tensor_scalar(w(22), pt("ss5")[:, :], 1.0 / 512, LN_EPS, ALU.mult, ALU.add), "pt_emptied_dve")
            V_(dve.reciprocal(w(22), w(22)), "s5_recip")
            for h in range(4):
                V_(dve.tensor_scalar(w(KP + h), w(K2 + h // 2), const(f"head{h % 2}"), None, ALU.mult), "k_padded")
            dve.wait_ge(E("s5_rstd"), 1)
            for m in range(4):
                V_(dve.scalar_tensor_tensor(w(UST + m).rearrange("p (n s) -> p s n", s=8),
                                            w(TS[m]).rearrange("p (s n) -> p s n", s=8), col("s5_out_gain_2", m),
                                            w(22).rearrange("p (s n) -> p s n", s=8), ALU.mult, ALU.mult), "y_s5")
            for i in range(2):
                V_(dve.tensor_tensor(w(QX[i]).rearrange("p (s n) -> p s n", s=8), w(Q2 + i).rearrange("p (s n) -> p s n", s=8),
                                     w(RETC)[:, 512 + P * i:640 + P * i].unsqueeze(1).to_broadcast([P, 8, P]), ALU.mult),
                   "qx_ready")
            for i in range(2):
                V_(dve.memset(w(STB[i]), 0.0), "state2_zero")
            for i in range(2):
                for hh in range(2):
                    h = 2 * i + hh
                    filled(dve, f"sc{h}")
                    V_(dve.tensor_tensor(g3(w(SCS[h])), g3(pt(f"sc{h}")[:, :]),
                                         w(RETC)[:, h * P:(h + 1) * P].unsqueeze(1).to_broadcast([P, 8, P]), ALU.mult),
                       "pt_emptied_dve")
                for n in range(16):
                    st = n // 2
                    if n % 2 == 0:
                        dve.wait_ge(E("kv_done"), 8 * i + st + 1)
                    if n >= 3 and n < 15:
                        dve.wait_ge(E("ro_step"), 7 * i + (n - 3) // 2 + 1)
                    for hh in range(2):
                        rows, cols = slice(64 * hh, 64 * hh + 64), hh * P
                        at = (n % 2) * 256 + (st % 2) * 512 + cols
                        if n < 15:
                            V_(dve.scalar_tensor_tensor(
                                w(STB[i])[rows, ((n + 1) % 4) * 256 + cols:((n + 1) % 4) * 256 + cols + P],
                                w(STB[i])[rows, (n % 4) * 256 + cols:(n % 4) * 256 + cols + P],
                                const("ret_chunk")[rows, i:i + 1], pt(f"kv{i}")[rows, at:at + P], ALU.mult, ALU.add), "state2")
                        else:
                            V_(dve.tensor_copy(c(TA), c(TB_)), "state2" if hh == 0 else "state2")
                V_(dve.tensor_copy(c(TA), c(TB_)), "pt_emptied_dve")
            for h in range(4):
                filled(dve, f"rm{h}")
                V_(dve.scalar_tensor_tensor(w(SCS[h]), pt(f"rm{h}")[:, :], -1.0 / P, w(SCS[h]), ALU.mult, ALU.add),
                   "pt_emptied_dve")
                filled(dve, f"rv{h}")
                V_(dve.tensor_scalar(w(KP + h), pt(f"rv{h}")[:, :], 1.0 / P, LN_EPS, ALU.mult, ALU.add), "pt_emptied_dve")
                V_(dve.reciprocal(w(KP + h), w(KP + h)), "ret_recip")
                dve.wait_ge(E("ret_sqrt"), h + 1)
                V_(dve.scalar_tensor_tensor(w(SCS[h]), w(SCS[h]), col("ret_gn_gain_2", h), w(KP + h), ALU.mult, ALU.mult))
                V_(dve.tensor_tensor(w(GATE + h), w(GATE + h), w(SCS[h]), ALU.mult), "y_ret")
            for m in range(8):
                filled(dve, f"p{m}")
                V_(dve.scalar_tensor_tensor(w(X + m), w(X + m), ALPHA, pt(f"p{m}")[:, :], ALU.mult, ALU.add), "pt_emptied_dve")
                add_x(dve, 0, m)
            for t in (1, 2):
                filled(dve, f"lm{t}")
                V_(dve.tensor_scalar(w(RSTD), pt(f"lm{t}")[:, :], 1.0 / D, None, ALU.mult), "pt_emptied_dve")
                for k in range(8):
                    V_(dve.tensor_tensor(w(X + k), w(X + k), w(RSTD), ALU.subtract), "centered")
                filled(dve, f"lv{t}")
                V_(dve.tensor_scalar(w(RSTD), pt(f"lv{t}")[:, :], 1.0 / D, LN_EPS, ALU.mult, ALU.add), "pt_emptied_dve")
                V_(dve.reciprocal(w(RSTD), w(RSTD)), "rstd_recip")
                dve.wait_ge(E("rstd_sqrt"), 3 + t)
                for k in range(8):
                    V_(dve.scalar_tensor_tensor(w(X + k), w(X + k), col(f"ln{t}_g_2", k), w(RSTD), ALU.mult, ALU.mult),
                       "ln_scaled")
                    if t == 1 and k > 0:
                        dve.wait_ge(E("x3_hi"), k)
                        V_(dve.tensor_tensor(lo(HLO, k - 1), w(X + k - 1), hi(H + k - 1).bitcast(F32), ALU.subtract), "ffn_rhs_split")
                if t == 1:
                    dve.wait_ge(E("x3_hi"), 8)
                    V_(dve.tensor_tensor(lo(HLO, 7), w(X + 7), hi(H + 7).bitcast(F32), ALU.subtract), "ffn_rhs_split")
                    ffn_dve(dve, 1, "ffn_conv_w_2", None, ALPHA)

        block = ctx.enter_context(nc.Block())

        @block.sync
        def _(sp):
            sp.dma_start(w(CB), a["c_rows"]).then_inc(E("c_in"), 16)
            sp.dma_start(par[:, :], a["vectors"]).then_inc(E("par_in"), 16)
            sp.dma_start(cst[:, :], a["const"]).then_inc(E("par_in"), 16)
            for q in range(4):
                sp.dma_start(W[:, X + 2 * q:X + 2 * q + 2, :], a["xT"][:, 2 * q:2 * q + 2, :]).then_inc(E(f"x_in{q}"), 16)
            for q in range(4):
                sp.dma_start(W[:, 16 + 4 * q:20 + 4 * q, :], a["w_mod"][:, 4 * q:4 * q + 4, :]).then_inc(E(f"mod_in{q}"), 16)
            sp.dma_start(bs[:, :, :], a["sgu_bias"]).then_inc(E("sgu_in"), 16)
            for r, (name, src, n) in enumerate(ring):
                at = ring_at[name]
                for pn, (other, _, m) in enumerate(ring[:r]):
                    if any((ring_at[other] + i) % NRING == (at + j) % NRING for i in range(m) for j in range(n)) \
                            and all(not any((ring_at[o2] + i) % NRING == (at + j) % NRING
                                            for i in range(m2) for j in range(n))
                                    for o2, _, m2 in ring[pn + 1:r]):
                        last = "vA1" if other == "vA" else other
                        sp.wait_ge(E("pt_filled"), place[last] + 1)
                sp.dma_start(W[:, wslot(name):wslot(name) + n, :], src).then_inc(E(f"ring{at % NRING}"), 16)
                if r == 0:
                    sp.dma_start(flat42[:, 1152:1920], a["lru_w"]).then_inc(E("sgu_in"), 16)
                    sp.dma_start(flat42[:, 0:1152], a["lora_w"]).then_inc(E("lora_w_in"), 16)
                    sp.dma_start(keep[:, :], a["keep"]).then_inc(E("keep_in"), 16)
                if r == 2:
                    sp.wait_ge(E("mod_head"), 16)
                    sp.dma_start(w(T)[:, 0:512], a["sgu_w"]).then_inc(E("sgu_in"), 16)
                    sp.dma_start(w(T + 1)[:, 0:512], a["sgu_ln"]).then_inc(E("sgu_in"), 16)
            after_core_sp(sp)
            mixer2_sp(sp)

        @block.gpsimd
        def _(pool):
            for m in range(16, 48):
                if m == 16:
                    pool.wait_ge(E("mod_head"), 16)
                if m >= 18:
                    pool.wait_ge(E("mod_tail"), m - 17)
                pool.dma_start(w(MODRING + m % 2), a["w_mod"][:, m, :]).then_inc(E(f"modring{m % 2}"), 16)
            core_pool(pool)
            pool.wait_ge(E("state_new"), 3 * NC)
            ffn_pool(pool, 0)
            mixer2_pool(pool)
            pool.wait_ge(E("y_ret"), 4)
            ffn_pool(pool, 1)

        @block.tensor
        def _(pe):
            pe.wait_ge(E("par_in"), 32)
            stats_matmuls(pe, "ss1", H, 8, const("ones"), ("squares", 0))
            linear(pe, "uA0", ring_weights("uA0"), range(H, H + 8), lambda: ring_wait(pe, "uA0"), ("h_ready", 0))
            for g in range(2):
                claim(pe, f"vA{g}")
                if g == 0:
                    ring_wait(pe, "vA")
                wv = W[:, wslot("vA"):wslot("vA") + 2, :].rearrange("p a (b n) -> p (a b) n", n=256)
                for t in range(4):
                    st = 4 * g + t
                    for k in range(8):
                        ins = pe.matmul(pt(f"vA{g}")[:, t * 256:t * 256 + 256], w(H + k)[:, st * P:(st + 1) * P],
                                        wv[:, k, :], start=(k == 0), stop=(k == 7), skip_group_check=True)
                ins.then_inc(E("pt_filled"), 1)
            hs = range(H, H + 8)

            def proj(name):
                linear(pe, name, ring_weights(name), hs, lambda: ring_wait(pe, name))

            for name in ("uA1", "xr0", "xr1", "xr2"):
                proj(name)
            for i in range(2):
                for hh in range(2):
                    nm = f"mx{i}{hh}"
                    claim(pe, nm)
                    if i == 0 and hh == 0:
                        pe.wait_ge(E("v_normed"), 2)
                        pe.wait_ge(E("spatial_masked"), 1)
                    for st in range(8):
                        ins = pe.matmul(pt(nm)[:, st * P:(st + 1) * P],
                                        W[:, V:V + 2, :].rearrange("p a (b n) -> p (a b) n", n=256)[:, st, i * P:(i + 1) * P],
                                        w(T)[:, (2 * i + hh) * P:(2 * i + hh + 1) * P], start=True, stop=True,
                                        skip_group_check=True)
                    ins.then_inc(E("pt_filled"), 1)
            for i in range(3):
                proj(f"yg{i}")
                for g, nm in enumerate(("ra", "ix")):
                    linear(pe, f"{nm}{i}", lambda k, g=g, i=i: lru_w[:, g, i, :], [XR + i],
                           lambda i=i: (pe.wait_ge(E("pt_emptied_dve"), ordinal[f"xr{i}"]), pe.wait_ge(E("sgu_in"), 64)))
            for j in C_ORDER:
                proj(f"c{j}")
            for i in range(3):
                def lora(k, g, i=i):
                    return lora_w[:, g, i * P:(i + 1) * P]
                linear(pe, f"lw{i}", lambda k: lora(k, 0), [XWA], lambda: pe.wait_ge(E("lora_in_ready"), 2))
                linear(pe, f"la{i}", lambda k: lora(k, 1), [XWA])
                linear(pe, f"lg{i}", lambda k: lora(k, 2), [XG])
                stats_matmuls(pe, f"kks{i}", T1, 1, const("block_ones"), ("kk_squares", i))
                stats_matmuls(pe, f"bon{i}", T2, 1, const("block_ones"), ("bonus_products", i))
            core_pe(pe)
            after_core_pe(pe)
            mixer2_pe(pe)

        @block.scalar
        def _(act):
            act.wait_ge(E("c_in"), 16)
            did(act, act.activation(w(CB), w(CB), ACT.Silu), "c_act")
            for k in range(8):
                act.wait_ge(E(f"x_in{k // 2}"), 16)
                did(act, act.activation(w(H + k), w(X + k), ACT.Square), "squares")
            act.wait_ge(E("rstd_recip"), 1)
            did(act, act.activation(w(RSTD), w(RSTD), ACT.Sqrt), "rstd_sqrt")
            for k in range(8):
                act.wait_ge(E("h_scaled"), k + 1)
                did(act, act.activation(w(H + k), w(H + k), ACT.Identity, bias=small(MOD + k)), "h_ready")

            for nm, dst in (("uA0", U), ("vA0", V), ("vA1", V + 1), ("uA1", U + 1)):
                filled(act, nm)
                emptied(act, act.activation(w(dst), pt(nm)[:, :], ACT.Gelu_apprx_tanh), nm, "act")
            for i in range(3):
                filled(act, f"xr{i}")
                did(act, act.activation(w(XR + i), pt(f"xr{i}")[:, :], ACT.Identity, bias=col("lru_conv_b", i),
                                        scale=col("lru_conv_w", 9 + i)), "xr_first")
                if i == 0:
                    act.wait_ge(E("v_var"), 1)
                    did(act, act.activation(small(STAT + 8, 8), small(STAT + 8, 8), ACT.Sqrt), "v_sqrt")
            for i in range(3):
                if i == 0:
                    act.wait_ge(E("lam_abs"), 1)
                    did(act, act.activation(small(CLRU, 3), small(CLRU, 3), ACT.Exp, scale=-1.0), "act_step")
                    did(act, act.activation(small(CLRU, 3), small(CLRU, 3), ACT.Ln, bias=1.0), "lam_ln")
                filled(act, f"yg{i}")
                emptied(act, act.activation(w(G + i), pt(f"yg{i}")[:, :], ACT.Gelu_apprx_tanh), f"yg{i}", "act")
                if i > 0:
                    act.wait_ge(E("y_b"), i)
                filled(act, f"ra{i}")
                emptied(act, act.activation(w(T), pt(f"ra{i}")[:, :], ACT.Sigmoid, bias=col("lru_b_a", i)), f"ra{i}", "act")
                filled(act, f"ix{i}")
                emptied(act, act.activation(w(T + 1), pt(f"ix{i}")[:, :], ACT.Sigmoid, bias=col("lru_b_x", i)), f"ix{i}", "act")
                act.wait_ge(E("clru"), 1)
                did(act, act.activation(w(T + 2), w(T), ACT.Tanh, scale=small(NCLRU + i)), "act_step")
                did(act, act.activation(w(T), w(T), ACT.Exp, scale=small(CLRU + i)), "act_step")
                did(act, act.activation(w(30), w(T), ACT.Square), "lru_a2")
                act.wait_ge(E("lru_gap"), i + 1)
                did(act, act.activation(w(T + 2), w(T + 2), ACT.Sqrt), "lru_root")
            dst = {9: XWA, 10: XG}
            for j in range(9):
                dst[j] = RR + j
            for n, j in enumerate(C_ORDER):
                filled(act, f"c{j}")
                if j == 0:
                    act.wait_ge(E("y_b"), 3)
                if j == 8:
                    act.wait_ge(E("mod_tail"), 32)
                did(act, act.activation(w(dst[j]), pt(f"c{j}")[:, :], ACT.Copy, scale=small(OMM + j)), "c_first")
                if j == 0:
                    act.wait_ge(E("pt_emptied_dve"), ordinal["c10"])
                    did(act, act.activation(w(XWA)[0:64], w(XWA)[0:64], ACT.Tanh), "lora_in_ready")
                    did(act, act.activation(w(XG), w(XG), ACT.Sigmoid), "lora_in_ready")
            for i in range(3):
                if i > 0:
                    act.wait_ge(E("pt_emptied_dve"), ordinal[f"bon{i - 1}"])
                filled(act, f"lw{i}")
                emptied(act, act.activation(w(T1), pt(f"lw{i}")[:, :], ACT.Sigmoid, bias=col("rwkv_w0", i)), f"lw{i}", "act")
                filled(act, f"la{i}")
                emptied(act, act.activation(w(T2), pt(f"la{i}")[:, :], ACT.Sigmoid, bias=col("rwkv_a0", i)), f"la{i}", "act")
                filled(act, f"lg{i}")
                emptied(act, act.activation(w(GG[i]), pt(f"lg{i}")[:, :], ACT.Copy), f"lg{i}", "act")
                act.wait_ge(E("decay_logs"), i + 1)
                did(act, act.activation(small(PMID + 8 * i, 8), small(PMID + 8 * i, 8), ACT.Exp), "act_step")
                did(act, act.activation(w(T4), w(T4), ACT.Exp), "act_step")
                did(act, act.activation(w(T1), w(T5), ACT.Square), "kk_squares")
                act.wait_ge(E("kk_recip"), i + 1)
                did(act, act.activation(w(T1), w(T1), ACT.Sqrt), "kk_norm")
                act.wait_ge(E("z_ready"), i + 1)
                did(act, act.activation(w(T1), w(T3), ACT.Exp), "p_pos")
                did(act, act.activation(w(T4), w(T3), ACT.Exp, scale=-1.0), "p_neg")
                did(act, act.activation(small(PEND + 8 * i, 8), w(T1)[:, CH - 1::CH], ACT.Copy), "p_end")
            core_act(act)
            after_core_act(act)
            mixer2_act(act)

        @block.vector
        def _(dve):
            def V_(ins, name="dve_step"):
                return did(dve, ins, name)

            dve.wait_ge(E("c_act"), 1)
            for m in range(16):
                if m == 12:
                    filled(dve, "ss1")
                    V_(dve.tensor_scalar(w(RSTD), pt("ss1")[:, :], 1.0 / D, EPS, ALU.mult, ALU.add), "pt_emptied_dve")
                    V_(dve.reciprocal(w(RSTD), w(RSTD)), "rstd_recip")
                dve.wait_ge(E(f"mod_in{m // 4}"), 16)
                V_(dve.tensor_tensor_reduce(w(16 + m), w(16 + m), w(CB), 1.0, 0.0, ALU.mult, ALU.add, small(MOD + m)),
                   "mod_head")
            dve.wait_ge(E("par_in"), 32)
            V_(dve.tensor_tensor(small(MOD, 16), small(MOD, 16), col("b_mod", 0, 16), ALU.add))
            V_(dve.scalar_tensor_tensor(small(G1, 8), small(MOD + 8, 8), 1.0, col("norm_mix", 0, 8), ALU.add, ALU.mult))
            V_(dve.tensor_scalar(small(OMM, 11), col("rwkv_mu", 0, 11), -1.0, 1.0, ALU.mult, ALU.add))
            V_(dve.tensor_scalar(small(OMKA, 3), col("rwkv_k_a", 0, 3), -1.0, 1.0, ALU.mult, ALU.add))
            V_(dve.tensor_scalar(small(NCLRU, 3), col("lru_lambda", 0, 3), -1.0, None, ALU.mult))
            V_(dve.tensor_tensor(small(CLRU, 3), small(NCLRU, 3), col("lru_lambda", 0, 3), ALU.max), "lam_abs")
            V_(dve.tensor_scalar(small(NCLRU, 3), small(NCLRU, 3), 0.0, None, ALU.max))
            dve.wait_ge(E("rstd_sqrt"), 1)
            for k in range(8):
                V_(dve.scalar_tensor_tensor(w(H + k), w(X + k), small(G1 + k), w(RSTD), ALU.mult, ALU.mult), "h_scaled")

            tail = [16]

            def mod_tail(n):
                for m in range(tail[0], min(tail[0] + n, 48)):
                    dve.wait_ge(E(f"modring{m % 2}"), 16 * ((m - 16) // 2 + 1))
                    V_(dve.tensor_tensor_reduce(w(MODRING + m % 2), w(MODRING + m % 2), w(CB), 1.0, 0.0, ALU.mult,
                                                ALU.add, small(MOD + m)), "mod_tail")
                tail[0] = min(tail[0] + n, 48)

            dve.wait_ge(E("sgu_in"), 64)
            V_(dve.tensor_tensor(w(T)[:, 0:512].rearrange("p (h t) -> p h t", h=4),
                                 w(T)[:, 0:512].rearrange("p (h t) -> p h t", h=4),
                                 const("causal").unsqueeze(1).to_broadcast([P, 4, P]), ALU.mult), "spatial_masked")
            dve.wait_ge(E("pt_emptied_act"), ordinal["vA1"])
            vv = W[:, V:V + 2, :].rearrange("p a (b n) -> p (a b) n", n=256)
            for st in range(8):
                V_(dve.bn_stats(small(STAT + 16 + 6 * st, 6), vv[:, st, :]))
                V_(dve.bn_aggr(small(STAT + 64 + 2 * st, 2), small(STAT + 16 + 6 * st, 6)))
            mv = small(STAT + 64, 16).rearrange("p (s two) -> p s two", two=2)
            V_(dve.tensor_scalar(small(STAT + 8, 8), mv[:, :, 1], LN_EPS, None, ALU.add))
            V_(dve.reciprocal(small(STAT + 8, 8), small(STAT + 8, 8)), "v_var")
            dve.wait_ge(E("v_sqrt"), 1)
            for st in range(8):
                V_(dve.tensor_scalar(vv[:, st, :], vv[:, st, :], mv[:, st, 0:1], small(STAT + 8 + st), ALU.subtract, ALU.mult))
            for op, at in ((ALU.mult, 0), (ALU.add, 256)):
                V_(dve.tensor_tensor(vv, vv, w(T + 1)[:, at:at + 256].unsqueeze(1).to_broadcast([P, 8, 256]), op), "v_normed")

            def conv_taps(dst, src, name, weights, release):
                for j, c in enumerate(weights):
                    V_(dve.scalar_tensor_tensor(dst[:, j + 1:], src[:, :S - j - 1], c, dst[:, j + 1:], ALU.mult, ALU.add),
                       release if j == len(weights) - 1 else "dve_step")

            for i in range(3):
                dve.wait_ge(E("xr_first"), i + 1)
                conv_taps(w(XR + i), pt(f"xr{i}"), None,
                          [col("lru_conv_w", 3 * j + i) for j in (2, 1, 0)], "pt_emptied_dve")
                mod_tail(1)
            for i in range(2):
                for hh in range(2):
                    nm = f"mx{i}{hh}"
                    rows = slice(64 * hh, 64 * hh + 64)
                    filled(dve, nm)
                    if hh == 0:
                        dve.wait_ge(E("pt_emptied_act"), 4)
                    V_(dve.tensor_tensor(w(T + 2)[rows].rearrange("p (c t) -> p c t", t=P),
                                         pt(nm)[rows].rearrange("p (c t) -> p c t", t=P),
                                         bs[rows, i, :].unsqueeze(1).to_broadcast([64, 8, P]), ALU.add), "pt_emptied_dve")
                    V_(dve.tensor_tensor(w(U + i)[rows], w(U + i)[rows], w(T + 2)[rows], ALU.mult), "dve_step")
                    mod_tail(1)
            for i in range(3):
                if i == 0:
                    dve.wait_ge(E("lam_ln"), 1)
                    V_(dve.tensor_tensor(small(NCLRU, 3), small(NCLRU, 3), small(CLRU, 3), ALU.add))
                    V_(dve.tensor_scalar(small(CLRU, 3), small(NCLRU, 3), -LRU_C, None, ALU.mult))
                    V_(dve.tensor_scalar(small(NCLRU, 3), small(NCLRU, 3), LRU_C, None, ALU.mult), "clru")
                dve.wait_ge(E("lru_a2"), i + 1)
                V_(dve.scalar_tensor_tensor(w(T + 2), w(30), 1.0, w(T + 2), ALU.add, ALU.mult), "lru_gap")
                V_(dve.tensor_tensor(w(T + 1), w(T + 1), w(XR + i), ALU.mult))
                dve.wait_ge(E("lru_root"), i + 1)
                V_(dve.tensor_tensor(w(T + 1), w(T + 1), w(T + 2), ALU.mult))
                V_(dve.tensor_tensor_scan(w(T + 1), w(T), w(T + 1), 0.0, ALU.mult, ALU.add))
                V_(dve.tensor_tensor(w(G + i), w(G + i), w(T + 1), ALU.mult), "y_b")
                mod_tail(3)
            dst = {9: XWA, 10: XG}
            for j in range(9):
                dst[j] = RR + j
            for n, j in enumerate(C_ORDER):
                dve.wait_ge(E("c_first"), n + 1)
                d = w(dst[j])
                V_(dve.scalar_tensor_tensor(d[:, 1:], pt(f"c{j}")[:, :S - 1], col("rwkv_mu", j), d[:, 1:], ALU.mult, ALU.add),
                   "pt_emptied_dve")
                mod_tail(2)
            mod_tail(32)
            V_(dve.tensor_tensor(small(MOD + 16, 32), small(MOD + 16, 32), col("b_mod", 16, 32), ALU.add), "dve_step")
            V_(dve.scalar_tensor_tensor(small(G2, 8), small(MOD + 32, 8), 1.0, col("norm_ffn", 0, 8), ALU.add, ALU.mult))
            for i in range(3):
                r, k, v = w(RR + i), w(KK + i), w(VV + i)
                dve.wait_ge(E("pt_emptied_act"), ordinal[f"lw{i}"])
                V_(dve.tensor_scalar(w(T1), w(T1), -float(np.exp(-0.5)), None, ALU.mult))
                one = const("ones")
                for c in range(NC):
                    V_(dve.tensor_tensor_scan(w(T3)[:, c * CH:(c + 1) * CH], one, w(T1)[:, c * CH:(c + 1) * CH], 0.0,
                                              ALU.mult, ALU.add))
                cum = w(T3).rearrange("p (c t) -> p c t", t=CH)
                V_(dve.tensor_copy(small(PMID + 8 * i, 8), w(T3)[:, CH // 2 - 1::CH]))
                V_(dve.tensor_tensor(cum, cum, small(PMID + 8 * i, 8).unsqueeze(2).to_broadcast([P, NC, CH]), ALU.subtract))
                V_(dve.tensor_tensor(w(T4), w(T3), w(T1), ALU.subtract))
                V_(dve.tensor_scalar(w(T5), k, col("rwkv_k_k", i), None, ALU.mult), "decay_logs")
                filled(dve, f"kks{i}")
                V_(dve.tensor_scalar(w(T1), pt(f"kks{i}")[:, :], 1e-24, None, ALU.max), "pt_emptied_dve")
                V_(dve.reciprocal(w(T1), w(T1)), "kk_recip")
                dve.wait_ge(E("kk_norm"), i + 1)
                V_(dve.tensor_tensor(w(T5), w(T5), w(T1), ALU.mult))
                V_(dve.tensor_tensor(w(Z + i), w(T5), w(T4), ALU.mult), "z_ready")
                V_(dve.tensor_tensor(w(T5), w(T5), w(T2), ALU.mult))
                V_(dve.tensor_scalar(w(T2), w(T2), col("rwkv_k_a", i), small(OMKA + i), ALU.mult, ALU.add))
                V_(dve.tensor_tensor(k, k, w(T2), ALU.mult))
                V_(dve.scalar_tensor_tensor(w(T2), r, col("rwkv_r_k", i), k, ALU.mult, ALU.mult), "bonus_products")
                dve.wait_ge(E("p_pos"), i + 1)
                V_(dve.tensor_tensor(r, r, w(T1), ALU.mult))
                dve.wait_ge(E("p_neg"), i + 1)
                V_(dve.tensor_tensor(w(B + i), w(T5), w(T4), ALU.mult))
                V_(dve.tensor_tensor(k, k, w(T4), ALU.mult))
                filled(dve, f"bon{i}")
                V_(dve.tensor_tensor(w(BV + i), pt(f"bon{i}")[:, :], v, ALU.mult), "pt_emptied_dve")
            core_dve(dve)
            after_core_dve(dve)
            mixer2_dve(dve)


def second_arrays(g, tiles, spread):
    def stack(top, bottom):
        both = np.concatenate([top.transpose(1, 0, 2), bottom.transpose(1, 0, 2)], 0)
        return both.reshape(P, -1)

    def rows(v):
        return np.concatenate([v.T, v.T], 0)

    bre, bim = g["s5_b_re_2"][0], g["s5_b_im_2"][0]
    cre, cim = g["s5_c_re_2"][0].transpose(0, 2, 1), g["s5_c_im_2"][0].transpose(0, 2, 1)
    cols = np.concatenate([rows(g["s5_lambda_re_2"][0]), rows(g["s5_lambda_im_2"][0]), spread(g["s5_log_step_2"][0]),
                           np.tile(g["s5_d_2"][0].reshape(S5_G, 16).T, (8, 1))], 1)
    bc = np.concatenate([stack(bre, bim), stack(bim, bre), stack(cre, cim), stack(cim, cre)], 1).reshape(P, 2, 1024)
    w_in = g["w_in_2"][0]
    up = g["ffn_w_up_2"][0]
    glu = tiles(g["s5_glu_w_2"][0]).transpose(1, 0, 2).reshape(P, 2, 1024)
    return {
        "w_in_2": tiles(w_in), "w_v_2": w_in[:, 1024:1536].reshape(8, P, 512).transpose(1, 0, 2).reshape(P, 4, 1024),
        "s5_cols": cols, "s5_bc": bc, "w_glu": glu, "w_out_2": tiles(g["w_out_2"][0]),
        "w_up_2": np.stack([tiles(up[:, :FF]), tiles(up[:, FF:])], 2).reshape(FT, P, 2, D),
        "w_down_2": tiles(g["ffn_w_down_2"][0]),
    }


def kernel(**inputs):
    import concourse.bacc as bacc
    from concourse.bass_utils import run_bass_kernel_spmd

    g = {k: np.asarray(v) for k, v in inputs.items()}

    def tiles(w, n=P):
        k, m = w.shape
        return np.ascontiguousarray(w.reshape(k // P, P, m // n, n).transpose(2, 1, 0, 3)).reshape(m // n, P, k // P * n)

    vec = np.zeros((P, NVEC), np.float32)
    for name, n in VECTORS:
        vec[:, COL[name]:COL[name] + n] = g[name].reshape(n, P).T

    def spread(v):
        return np.ascontiguousarray(np.broadcast_to(v, (P,) + v.shape))

    lru = np.zeros((P, 2, 3, P), np.float32)
    for n, name in enumerate(("lru_w_a", "lru_w_x")):
        for b in range(6):
            o = 64 * (b % 2)
            lru[o:o + 64, n, b // 2, o:o + 64] = g[name][0, b]
    lora = np.zeros((P, 3, 384), np.float32)
    lora[:64, 0] = g["rwkv_w2"][0]
    lora[64:, 1] = g["rwkv_a2"][0]
    lora[:, 2] = g["rwkv_g2"][0]
    w_up = g["ffn_w_up"][0]
    w_up = np.stack([tiles(w_up[:, :FF]), tiles(w_up[:, FF:])], 2).reshape(FT, P, 2, D)
    w_in = g["w_in"][0]
    arrays = {
        "xT": g["x"][0].T.reshape(DT, P, S).transpose(1, 0, 2), "c_rows": spread(g["c"][0]), "vectors": vec,
        "w_mod": g["w_mod"][0].T.reshape(48, P, D).transpose(1, 0, 2),
        "w_in": tiles(w_in), "w_v": w_in[:, 256:512].reshape(8, P, 256).transpose(1, 0, 2).reshape(P, 2, 1024),
        "sgu_w": g["sgu_w"][0].transpose(2, 0, 1).reshape(P, 512),
        "sgu_ln": spread(np.concatenate([g["sgu_ln_g"][0], g["sgu_ln_b"][0]])),
        "sgu_bias": np.repeat(g["sgu_b"][0].reshape(2, 2, P).transpose(1, 0, 2), 64, axis=0),
        "lru_w": lru.reshape(P, 768), "lora_w": lora.reshape(P, 1152), "w_out": tiles(g["w_out"][0]), "w_up": w_up, "w_down": tiles(g["ffn_w_down"][0]),
    }
    arrays.update(shape_constants())
    arrays.update(second_arrays(g, tiles, spread))
    arrays = {k: np.ascontiguousarray(v) for k, v in arrays.items()}

    nc = bacc.Bacc("TRN2", target_bir_lowering=False, num_devices=1)
    a = {}
    for name, v in arrays.items():
        a[name] = nc.dram_tensor(f"in_{name}", v.shape, mybir.dt.from_np(v.dtype), kind="ExternalInput").ap()
    for name in ("u_scratch", "y_scratch"):
        a[name] = nc.dram_tensor(name, (512, S), F32).ap()
    a["out"] = nc.dram_tensor("out_xT", (P, DT, S), F32, kind="ExternalOutput").ap()
    build(nc, a)
    r = run_bass_kernel_spmd(nc, [{f"in_{k}": v for k, v in arrays.items()}], core_ids=[0])
    y = r.results[0]["out_xT"]
    return np.ascontiguousarray(y.transpose(1, 0, 2).reshape(D, S).T)[None]
```
